# Optimizing a Trainium2 kernel written in Bass

```python
import math
import jax, jax.numpy as jnp
from jax import lax
import numpy as np

D_MODEL = 2048
BATCH = 1
SEQ = 256
DEPTH = 1

GRID_W = 64
N_DIFF_HEADS = 8
DIFF_QK_DIM = 64
DIFF_V_DIM = 2 * DIFF_QK_DIM
DIFF_QK_COLS = N_DIFF_HEADS * 2 * DIFF_QK_DIM
DIFF_WIDTH = N_DIFF_HEADS * DIFF_V_DIM
Q_BLOCK = 128
N_NA_HEADS = 8
NA_HEAD_DIM = 128
NA_WIDTH = N_NA_HEADS * NA_HEAD_DIM
NA_KR_MAX = 8
NA_KC = 16
NA_SPAN = 2 * NA_KC
IN_COLS = 2 * DIFF_QK_COLS + DIFF_WIDTH + 3 * NA_WIDTH + 2 * D_MODEL
D_FF = 5632
CONV_W = 3
LN_EPS = 1e-5
RMS_EPS = 1e-5
DEEPNORM_ALPHA = (2.0 * DEPTH) ** 0.25
DEEPNORM_BETA = (8.0 * DEPTH) ** -0.25

kernel_name = "hybrid_diffattn_natten_convffn_deepnorm"

def layer_norm(x, g, b):
    xf = x.astype(jnp.float32)
    mu = jnp.mean(xf, -1, keepdims=True)
    var = jnp.mean(jnp.square(xf - mu), -1, keepdims=True)
    return ((xf - mu) * lax.rsqrt(var + LN_EPS) * g.astype(jnp.float32) + b.astype(jnp.float32)).astype(x.dtype)

def rms_norm(x, g):
    xf = x.astype(jnp.float32)
    ms = jnp.mean(jnp.square(xf), -1, keepdims=True)
    return (xf * lax.rsqrt(ms + RMS_EPS) * g.astype(jnp.float32)).astype(x.dtype)

def alibi_slopes(n):
    return np.array([2.0 ** (-8.0 * (i + 1) / n) for i in range(n)], dtype=np.float32)

def diff_attention(q1, q2, k1, k2, v, lam):
    B, H, S, _ = q1.shape
    nblk = S // Q_BLOCK
    scale = DIFF_QK_DIM ** -0.5
    slopes = jnp.asarray(alibi_slopes(H))[:, None, None]
    kpos = jnp.arange(S, dtype=jnp.int32)

    def to_blocks(q):
        return q.reshape(B, H, nblk, Q_BLOCK, q.shape[-1]).transpose(2, 0, 1, 3, 4)

    def one_block(args):
        q1b, q2b, start = args
        qpos = start + jnp.arange(Q_BLOCK, dtype=jnp.int32)
        bias = -slopes * jnp.abs(qpos[:, None] - kpos[None, :]).astype(jnp.float32)
        s1 = jnp.einsum('bhqd,bhkd->bhqk', q1b, k1).astype(jnp.float32) * scale + bias
        s2 = jnp.einsum('bhqd,bhkd->bhqk', q2b, k2).astype(jnp.float32) * scale + bias
        a = jax.nn.softmax(s1, axis=-1) - lam * jax.nn.softmax(s2, axis=-1)
        return jnp.einsum('bhqk,bhkd->bhqd', a.astype(v.dtype), v)

    starts = jnp.arange(nblk, dtype=jnp.int32) * Q_BLOCK
    out = lax.map(one_block, (to_blocks(q1), to_blocks(q2), starts))
    return out.transpose(1, 2, 0, 3, 4).reshape(B, H, S, v.shape[-1])

def neighbourhood_attention(q, k, v, rpb):
    B, H, S, d = q.shape
    rows = S // GRID_W
    kr = min(NA_KR_MAX, rows)
    nb = GRID_W // NA_KC
    scale = d ** -0.5
    r = np.arange(rows)
    row_start = np.clip(r - kr // 2, 0, rows - kr)
    dr_idx = row_start[:, None] + np.arange(kr)[None, :] - r[:, None] + (NA_KR_MAX - 1)
    c = np.arange(GRID_W)
    col_start = np.clip(c - NA_KC // 2, 0, GRID_W - NA_KC)
    span_start = np.clip(np.arange(nb) * NA_KC - NA_KC // 2, 0, GRID_W - NA_SPAN)
    span_cols = span_start[:, None] + np.arange(NA_SPAN)[None, :]
    key_col = span_cols[c // NA_KC]
    col_valid = (key_col >= col_start[:, None]) & (key_col < col_start[:, None] + NA_KC)
    dc_idx = np.clip(key_col - c[:, None] + (NA_KC - 1), 0, 2 * NA_KC - 2)
    bias = rpb[:, dr_idx[:, None, :, None], dc_idx[None, :, None, :]].astype(jnp.float32)
    bias = jnp.where(jnp.asarray(col_valid)[None, None, :, None, :], bias, -jnp.inf)
    bias_rows = bias.transpose(1, 0, 2, 3, 4).reshape(rows, H, nb, NA_KC, kr, NA_SPAN)

    q_rows = q.reshape(B, H, rows, nb, NA_KC, d).transpose(2, 0, 1, 3, 4, 5)
    k_grid = k.reshape(B, H, rows, GRID_W, d)
    v_grid = v.reshape(B, H, rows, GRID_W, d)

    def one_row(args):
        q_row, bias_row, r0 = args
        k_strip = lax.dynamic_slice_in_dim(k_grid, r0, kr, axis=2)
        v_strip = lax.dynamic_slice_in_dim(v_grid, r0, kr, axis=2)
        k_blk = k_strip[:, :, :, span_cols]
        v_blk = v_strip[:, :, :, span_cols]
        s = jnp.einsum('bhnqd,bhrnkd->bhnqrk', q_row, k_blk).astype(jnp.float32) * scale + bias_row
        p = jax.nn.softmax(s, axis=(-2, -1))
        return jnp.einsum('bhnqrk,bhrnkd->bhnqd', p.astype(v.dtype), v_blk)

    out = lax.map(one_row, (q_rows, bias_rows, jnp.asarray(row_start, dtype=jnp.int32)))
    return out.transpose(1, 2, 0, 3, 4, 5).reshape(B, H, S, d)

def token_mixer(x, w_in, b_in, lam_q1, lam_k1, lam_q2, lam_k2, subln_g, rpb,
                w_branch_a, w_branch_b, w_out, lambda_init):
    B, S, _ = x.shape
    z = jnp.einsum('bsd,dc->bsc', x, w_in) + b_in
    splits = [int(i) for i in np.cumsum([DIFF_QK_COLS, DIFF_QK_COLS, DIFF_WIDTH,
                                         NA_WIDTH, NA_WIDTH, NA_WIDTH, D_MODEL])]
    qa, ka, va, qb, kb, vb, ga, gb = jnp.split(z, splits, axis=-1)

    qa = qa.reshape(B, S, N_DIFF_HEADS, 2, DIFF_QK_DIM).transpose(3, 0, 2, 1, 4)
    ka = ka.reshape(B, S, N_DIFF_HEADS, 2, DIFF_QK_DIM).transpose(3, 0, 2, 1, 4)
    va = va.reshape(B, S, N_DIFF_HEADS, DIFF_V_DIM).transpose(0, 2, 1, 3)
    lam = (jnp.exp(jnp.sum(lam_q1.astype(jnp.float32) * lam_k1.astype(jnp.float32)))
           - jnp.exp(jnp.sum(lam_q2.astype(jnp.float32) * lam_k2.astype(jnp.float32)))
           + lambda_init)
    oa = diff_attention(qa[0], qa[1], ka[0], ka[1], va, lam)
    oa = rms_norm(oa, subln_g) * (1.0 - lambda_init)
    oa = oa.transpose(0, 2, 1, 3).reshape(B, S, DIFF_WIDTH)

    def heads(t):
        return t.reshape(B, S, N_NA_HEADS, NA_HEAD_DIM).transpose(0, 2, 1, 3)
    ob = neighbourhood_attention(heads(qb), heads(kb), heads(vb), rpb)
    ob = ob.transpose(0, 2, 1, 3).reshape(B, S, NA_WIDTH)

    y = (jax.nn.sigmoid(ga) * jnp.einsum('bsc,cd->bsd', oa, w_branch_a)
         + jax.nn.sigmoid(gb) * jnp.einsum('bsc,cd->bsd', ob, w_branch_b))
    return jnp.einsum('bsd,de->bse', y, w_out)

def conv_ffn(x, w_up, conv_w, conv_b, w_down):
    S = x.shape[1]
    h = jnp.einsum('bsd,df->bsf', x, w_up)
    pad = CONV_W // 2
    hp = jnp.pad(h, ((0, 0), (pad, pad), (0, 0)))
    hc = conv_b + hp[:, 0:S] * conv_w[0]
    for i in range(1, CONV_W):
        hc = hc + hp[:, i:i + S] * conv_w[i]
    gate, val = jnp.split(hc, 2, axis=-1)
    return jnp.einsum('bsf,fd->bsd', jax.nn.gelu(gate, approximate=False) * val, w_down)

def setup_inputs(seed: int = 0) -> dict:
    key = jax.random.key(seed)
    ks = jax.random.split(key, 21)
    f32 = jnp.float32
    n = lambda k, shape, s: jax.random.normal(k, shape, f32) * s
    L = DEPTH
    return {
        "x": jax.random.normal(ks[0], (BATCH, SEQ, D_MODEL), f32),
        "w_in": n(ks[1], (L, D_MODEL, IN_COLS), D_MODEL ** -0.5),
        "b_in": n(ks[2], (L, IN_COLS), 0.02),
        "lam_q1": n(ks[3], (L, DIFF_QK_DIM), 0.1),
        "lam_k1": n(ks[4], (L, DIFF_QK_DIM), 0.1),
        "lam_q2": n(ks[5], (L, DIFF_QK_DIM), 0.1),
        "lam_k2": n(ks[6], (L, DIFF_QK_DIM), 0.1),
        "subln_g": 1.0 + n(ks[7], (L, DIFF_V_DIM), 0.02),
        "rpb": n(ks[8], (L, N_NA_HEADS, 2 * NA_KR_MAX - 1, 2 * NA_KC - 1), 0.02),
        "w_branch_a": n(ks[9], (L, DIFF_WIDTH, D_MODEL), DIFF_WIDTH ** -0.5),
        "w_branch_b": n(ks[10], (L, NA_WIDTH, D_MODEL), NA_WIDTH ** -0.5),
        "w_out": n(ks[11], (L, D_MODEL, D_MODEL), DEEPNORM_BETA * D_MODEL ** -0.5),
        "ln1_g": 1.0 + n(ks[12], (L, D_MODEL), 0.02),
        "ln1_b": n(ks[13], (L, D_MODEL), 0.02),
        "w_up": n(ks[14], (L, D_MODEL, 2 * D_FF), D_MODEL ** -0.5),
        "conv_w": n(ks[15], (L, CONV_W, 2 * D_FF), CONV_W ** -0.5),
        "conv_b": n(ks[16], (L, 2 * D_FF), 0.02),
        "w_down": n(ks[17], (L, D_FF, D_MODEL), DEEPNORM_BETA * D_FF ** -0.5),
        "ln2_g": 1.0 + n(ks[18], (L, D_MODEL), 0.02),
        "ln2_b": n(ks[19], (L, D_MODEL), 0.02),
    }

def reference(x, w_in, b_in, lam_q1, lam_k1, lam_q2, lam_k2, subln_g, rpb,
              w_branch_a, w_branch_b, w_out, ln1_g, ln1_b,
              w_up, conv_w, conv_b, w_down, ln2_g, ln2_b):
    for l in range(DEPTH):
        lambda_init = 0.8 - 0.6 * math.exp(-0.3 * l)
        h = token_mixer(x, w_in[l], b_in[l], lam_q1[l], lam_k1[l], lam_q2[l], lam_k2[l],
                        subln_g[l], rpb[l], w_branch_a[l], w_branch_b[l], w_out[l], lambda_init)
        x = layer_norm(DEEPNORM_ALPHA * x + h, ln1_g[l], ln1_b[l])
        f = conv_ffn(x, w_up[l], conv_w[l], conv_b[l], w_down[l])
        x = layer_norm(DEEPNORM_ALPHA * x + f, ln2_g[l], ln2_b[l])
    return x


_drawn_inputs = setup_inputs


def setup_inputs(seed=0):
    import zlib

    import numpy as np

    out = dict(_drawn_inputs(seed))
    spreads = {}
    factors = {'lam_q1': 8.0,
     'lam_k1': 6.632,
     'lam_q2': 34.297,
     'lam_k2': 3.084,
     'subln_g': 8.0,
     'rpb': 64.0,
     'ln1_g': 2.77,
     'conv_b': 6.401,
     'ln2_g': 8.067,
     'ln2_b': 8.287,
     'ln1_b': 6.197}
    for name, (base, spread) in spreads.items():
        noise = np.random.default_rng([zlib.crc32(name.encode()), seed]).standard_normal(out[name].shape)
        drawn = base * np.exp(spread * noise) if base else spread * noise
        out[name] = __import__('jax').numpy.asarray(drawn.astype(out[name].dtype))
    for name, factor in factors.items():
        out[name] = (out[name] * factor).astype(out[name].dtype)
    return out
```

```python
import math
from contextlib import ExitStack

import concourse.bass as bass
from concourse import mybir
from concourse.alu_op_type import AluOpType as ALU

ACT = mybir.ActivationFunctionType
AX = mybir.AxisListType
F32 = mybir.dt.float32
F32R = mybir.dt.float32r

P = 128
D_MODEL = 2048
SEQ = 256
TT = SEQ // P
KC = D_MODEL // P
HEADS = 8
QK_DIM = 64
HEAD = 128
WIDTH = HEADS * HEAD
GRID_W = 64
NA_KC = 16
RPB_R, RPB_C = 15, 31
D_FF = 5632
FC = D_FF // P
LN_EPS = 1e-5
RMS_EPS = 1e-5
ALPHA = 2.0 ** 0.25
LAMBDA_INIT = 0.8 - 0.6 * math.exp(0.0)
DIFF_SCALE = QK_DIM ** -0.5
NA_SCALE = HEAD ** -0.5
MASKED = -1.0e30

GROUP = 512
SUB = GROUP // P
PIECE_K = 2
RING = 4
START = 1
LEAD = RING - 1

PG = KC // PIECE_K
PB = WIDTH // P // PIECE_K
PF = FC // PIECE_K
G_QK, G_V, G_GATE = 0, 8, 12
G_END = 20
N_QK, N_V, N_GATE = 0, 64, 96
N_BRANCH, N_OUT, N_UP, N_DOWN, N_ALL = 160, 192, 224, 400, 488
PAIRS_UP = D_FF // GROUP

C_QA, C_VA, C_QB, C_VB, C_GATE = 0, 2048, 3072, 5120, 6144
T_BIN, T_LNG, T_LNB, T_CW, T_CB, T_ALL = 0, 80, 96, 112, 376, 464


def encoder_block(nc, x, w_in, b_in, lam_q1, lam_k1, lam_q2, lam_k2, subln_g, rpb, w_branch_a,
                  w_branch_b, w_out, ln1_g, ln1_b, w_up, conv_w, conv_b, w_down, ln2_g, ln2_b, out):
    ctx = ExitStack()
    with ctx:
        base = (nc.sbuf_base + 31) // 32 * 32

        def at(name, offset, shape, dtype=F32):
            return nc.alloc_sbuf_tensor_at(name, shape, dtype, offset=base + offset)

        def sem(name):
            return ctx.enter_context(nc.semaphore(name))

        piece_bytes = PIECE_K * GROUP * 4
        o = 0
        raw = at("raw", o, [P, RING, PIECE_K, GROUP]); o += RING * piece_bytes
        w_hi = at("w_hi", o, [P, RING, PIECE_K, GROUP], F32R); o += RING * piece_bytes
        w_lo = at("w_lo", o, [P, RING, PIECE_K, GROUP], F32R); o += RING * piece_bytes
        ident = at("ident", o, [P, P]); o += P * 4
        table = at("table", o, [P, T_ALL]); o += T_ALL * 4
        small = at("small", o, [P, 120]); o += 480
        r1 = o
        xT_hi = at("xT_hi", o, [P, KC, SEQ], F32R)
        xT_lo = at("xT_lo", o + 16384, [P, KC, SEQ], F32R)
        yT_hi = at("yT_hi", o, [P, KC, SEQ], F32R)
        yT_lo = at("yT_lo", o + 16384, [P, KC, SEQ], F32R)
        o += 32768
        qkT = at("qkT", o, [P, 4, HEADS, SEQ])
        obT_hi = at("obT_hi", o + 16384, [P, HEADS, SEQ], F32R)
        obT_lo = at("obT_lo", o + 24576, [P, HEADS, SEQ], F32R)
        o += 32768
        rel = at("rel", o, [P, HEADS, 6, GRID_W]); o += 12288
        dist = at("dist", o, [P, 384]); o += 1536
        ones = at("ones", o, [P, P]); o += 512
        sA = at("sA", o, [P, 2, TT, SEQ]); o += 4096
        sB = at("sB", o, [P, TT, SEQ]); o += 2048
        aT = at("aT", o, [P, TT, SEQ])
        flip = at("flip", o, [P, P]); o += 2048
        pT = at("pT", o, [P, TT, SEQ]); o += 2048
        hT_hi = at("hT_hi", r1, [P, FC, SEQ], F32R)
        hT_lo = at("hT_lo", r1 + FC * SEQ * 4, [P, FC, SEQ], F32R)
        assert o - r1 == 2 * FC * SEQ * 4
        ln1_nat = at("ln1_nat", r1 + (2 * FC - 16) * SEQ * 4, [P, 2, D_MODEL])
        r2 = o
        gate = at("gate", r2, [P, 2 * KC, SEQ])
        x_in = at("x_in", r2, [P, TT, D_MODEL])
        rel_rev = at("rel_rev", r2, [P, HEADS, 6, GRID_W])
        vbias = at("vbias", r2 + 16384, [P, 2, WIDTH])
        x1T_hi = at("x1T_hi", r2, [P, KC, SEQ], F32R)
        x1T_lo = at("x1T_lo", r2 + 16384, [P, KC, SEQ], F32R)
        ln2_nat = at("ln2_nat", r2, [P, 2, D_MODEL])
        o += 32768
        vN = at("vN", o, [P, TT, 2, WIDTH])
        res = at("res", o, [P, TT, D_MODEL])
        o += 16384
        r4 = o
        par = at("par", r4, [P, 5, P])
        lamv = at("lamv", r4 + 2560, [P, 4, QK_DIM])
        oaT_hi = at("oaT_hi", r4, [P, HEADS, SEQ], F32R)
        oaT_lo = at("oaT_lo", r4 + 8192, [P, HEADS, SEQ], F32R)
        x1f = at("x1f", r4, [P, 4, PIECE_K * SEQ])
        cg = at("cg", r4 + 8192, [P, SUB, SEQ])
        cv = at("cv", r4 + 12288, [P, SUB, SEQ])
        o += 16384
        stA = at("stA", o, [P, 2, SEQ])
        stQb = at("stQb", o + 2048, [P, SEQ])
        stV = at("stV", o + 3072, [P, 2, TT, HEAD])
        o += 5120
        assert base + o <= nc.sbuf_usable_end

        slope8 = small[:, 0:8]
        neg_max = small[:, 8:14]
        neg_maxs = small[:, 14:18]
        sums = small[:, 18:24]
        rsum = small[:, 24:30]
        coef = small[:, 30:32]
        lam_dot = small[:, 32:34]
        lam_exp = small[:, 34:36]
        lam_dif = small[:, 36:37]
        neg_lam = small[:, 37:38]
        subg = small[:, 38:39]
        subg8 = small[:, 39:40]
        stats = small[:, 40:88].rearrange("p (t g s) -> p t g s", t=TT, g=4)
        mv = small[:, 88:92].rearrange("p (t s) -> p t s", t=TT)
        std = small[:, 92:94]
        rstd = small[:, 94:96]
        eps_c = small[:, 96:97]
        oa = sB[:, 0, :]
        oa_rms = sA[:, 1, 1, :]
        oa_sq = sA[:, 1, 0, :]
        vpe = small[:, 98:100]
        shift = small[:, 100:102]

        ps = ctx.enter_context(nc.psum_tensor("ps", [P, 8, 512], F32))

        raw_loaded = [sem(f"raw_loaded{s}") for s in range(RING)]
        rounded = sem("rounded")
        residual = sem("residual")
        used = sem("used")
        banks_free = sem("banks_free")
        x_loaded = [sem(f"x_loaded{q}") for q in range(4)]
        ident_ready = sem("ident_ready")
        const_ready = sem("const_ready")
        consts_set = sem("consts_set")
        pool_steps = sem("pool_steps")
        par_loaded = sem("par_loaded")
        rel_loaded = sem("rel_loaded")
        rel_masked = sem("rel_masked")
        rel_flipped = sem("rel_flipped")
        rel_copied = sem("rel_copied")
        vbias_loaded = sem("vbias_loaded")
        lam_loaded = sem("lam_loaded")
        xt_ready = sem("xt_ready")
        xt_hi = sem("xt_hi")
        xt_lo = sem("xt_lo")
        par_turned = sem("par_turned")
        table_ready = sem("table_ready")
        dist_raw = sem("dist_raw")
        dist_ready = sem("dist_ready")
        lam_steps = sem("lam_steps")
        lam_exped = sem("lam_exped")
        staged_qk = sem("staged_qk")
        staged_v = sem("staged_v")
        scores_ready = sem("scores_ready")
        biased = sem("biased")
        maxed = sem("maxed")
        exped = sem("exped")
        soft = sem("soft")
        normed_a = sem("normed_a")
        normed_b = sem("normed_b")
        turned = sem("turned")
        aT_ready = sem("aT_ready")
        pT_ready = sem("pT_ready")
        pv_done = sem("pv_done")
        oa_copied = sem("oa_copied")
        squared = sem("squared")
        ms_ready = sem("ms_ready")
        ob_hi = sem("ob_hi")
        ob_lo = sem("ob_lo")
        oa_sqrt = sem("oa_sqrt")
        oa_steps = sem("oa_steps")
        oa_hi = sem("oa_hi")
        oa_lo = sem("oa_lo")
        gates_on = sem("gates_on")
        b_gated = sem("b_gated")
        a_gated = sem("a_gated")
        y_summed = sem("y_summed")
        y_hi = sem("y_hi")
        y_lo = sem("y_lo")
        res_loaded = sem("res_loaded")
        ln1_loaded = sem("ln1_loaded")
        ln2_loaded = sem("ln2_loaded")
        res_steps = sem("res_steps")
        stat_steps = sem("stat_steps")
        ln_steps = sem("ln_steps")
        ln_sqrt = sem("ln_sqrt")
        xn0_ready = sem("xn0_ready")
        xn1_ready = sem("xn1_ready")
        x1t_turned = sem("x1t_turned")
        x1_aff = sem("x1_aff")
        x1_hi = sem("x1_hi")
        x1_lo = sem("x1_lo")
        x1_nat = sem("x1_nat")
        g_mid = sem("g_mid")
        g_conv = sem("g_conv")
        g_act = sem("g_act")
        v_mid = sem("v_mid")
        v_conv = sem("v_conv")
        h_ready = sem("h_ready")
        h_hi = sem("h_hi")
        h_lo = sem("h_lo")
        out_ready = sem("out_ready")
        out_steps = sem("out_steps")
        out_stored = sem("out_stored")

        block = ctx.enter_context(nc.Block())

        def evacuated(g):
            return g + 3

        def pieces(weights):
            return weights.rearrange("(j a p) n -> j p a n", a=PIECE_K, p=P)

        w_in_p, w_a_p, w_b_p = pieces(w_in[0]), pieces(w_branch_a[0]), pieces(w_branch_b[0])
        w_out_p, w_up_p, w_down_p = pieces(w_out[0]), pieces(w_up[0]), pieces(w_down[0])

        @block.sync
        def _(sp):
            for q in range(4):
                sp.dma_start(x_in[:, :, q * 512:(q + 1) * 512],
                             x[0].rearrange("(t p) d -> p t d", p=P)[:, :, q * 512:(q + 1) * 512]
                             ).then_inc(x_loaded[q], 16)

            def load_group(src, count, n0, col, slot0=0):
                for j in range(count):
                    slot = (slot0 + j) % RING
                    sp.wait_ge(residual, n0 + j + 1)
                    sp.dma_start(raw[:, slot], src[j][:, :, bass.ds(col, GROUP)]
                                 ).then_inc(raw_loaded[slot], 16)

            with sp.Fori(0, 2) as a:
                with sp.Fori(0, 2) as b:
                    for u in range(2):
                        load_group(w_in_p, PG, N_QK + a * 32 + b * 16 + u * PG,
                                   C_QA + a * C_QB + b * WIDTH + u * GROUP)
            with sp.Fori(0, 2) as a:
                for u in range(2):
                    load_group(w_in_p, PG, N_V + a * 16 + u * PG, C_VA + a * (C_VB - C_VA) + u * GROUP)
            with sp.Fori(0, 8) as g:
                load_group(w_in_p, PG, N_GATE + g * PG, C_GATE + g * GROUP)
            with sp.Fori(0, 4) as c:
                load_group(w_b_p, PB, N_BRANCH + c * 8, c * GROUP)
                load_group(w_a_p, PB, N_BRANCH + c * 8 + PB, c * GROUP)
            with sp.Fori(0, 4) as c:
                load_group(w_out_p, PG, N_OUT + c * PG, c * GROUP)
            with sp.Fori(0, PAIRS_UP) as i:
                load_group(w_up_p, PG, N_UP + i * 16, i * GROUP)
                load_group(w_up_p, PG, N_UP + i * 16 + PG, D_FF + i * GROUP)
            with sp.Fori(0, 2) as i:
                for u in range(2):
                    load_group(w_down_p, PF, N_DOWN + i * 2 * PF + u * PF, i * 2 * GROUP + u * GROUP,
                               slot0=u * PF % RING)
            for s in range(8):
                t, q = s // 4, s % 4
                sp.wait_ge(out_ready, s + 1)
                sp.dma_start(out[0, t * P:(t + 1) * P, q * 512:(q + 1) * 512],
                             res[:, t, q * 512:(q + 1) * 512]).then_inc(out_stored, 16)
            sp.wait_ge(out_stored, 8 * 16)

        @block.gpsimd
        def _(pool):
            pool.memset(ident[:, :], 0.0).then_inc(pool_steps, 1)
            pool.wait_ge(pool_steps, 1)
            pool.affine_select(out=ident[:, :], in_=ident[:, :], compare_op=ALU.not_equal, fill=1.0,
                               base=0, pattern=[[-1, P]], channel_multiplier=1).then_inc(ident_ready, 1)
            pool.memset(ones[:, :], 1.0 / HEAD).then_inc(const_ready, 1)
            pool.iota(dist[:, :], pattern=[[-1, 384]], base=P, channel_multiplier=1,
                      allow_small_or_imprecise_dtypes=True).then_inc(dist_raw, 1)
            rows = lambda v: v.rearrange("(c p) -> c p", p=P)
            pool.dma_start(par[0:80, 0, :], rows(b_in[0])).then_inc(par_loaded, 16)
            pool.dma_start(par[80:96, 0, :], rows(ln1_g[0])).then_inc(par_loaded, 16)
            pool.dma_start(par[96:112, 0, :], rows(ln1_b[0])).then_inc(par_loaded, 16)
            for k in range(3):
                pool.dma_start(par[0:88, 1 + k, :], rows(conv_w[0, k])).then_inc(par_loaded, 16)
            pool.dma_start(par[0:88, 4, :], rows(conv_b[0])).then_inc(par_loaded, 16)
            for k, v in enumerate((lam_q1, lam_q2, lam_k1, lam_k2)):
                pool.dma_start(lamv[:, k, :], v[0].partition_broadcast(P)).then_inc(lam_loaded, 16)
            pool.dma_start(subg, subln_g[0].rearrange("(p a) -> p a", a=1)).then_inc(lam_loaded, 16)
            for s, c in enumerate((C_VA, C_VB)):
                pool.dma_start(vbias[:, s, :], b_in[0, c:c + WIDTH].partition_broadcast(P)
                               ).then_inc(vbias_loaded, 16)
            pool.memset(flip[:, :], 0.0).then_inc(pool_steps, 1)
            for k, total in enumerate((GRID_W - 1, 3 * GRID_W - 1)):
                pool.wait_ge(pool_steps, 2 + k)
                pool.affine_select(out=flip[:, :], in_=flip[:, :], compare_op=ALU.not_equal, fill=1.0,
                                   base=-total, pattern=[[1, P]], channel_multiplier=1
                                   ).then_inc(pool_steps, 1)
            pool.wait_ge(xt_ready, KC // 2)
            for b in range(2):
                for h in range(HEADS):
                    src = bass.AP(rpb.tensor,
                                  h * RPB_R * RPB_C + (5 - b) * RPB_C + NA_KC - 1 - (GRID_W - 1),
                                  [[1, GRID_W], [RPB_C, 6], [1, GRID_W]])
                    pool.dma_start(rel_rev[b * 64:(b + 1) * 64, h], src).then_inc(rel_loaded, 16)
            pool.wait_ge(rel_loaded, 16 * 2 * HEADS)
            pool.wait_ge(pool_steps, 4)
            for b in range(2):
                if b:
                    pool.wait_ge(rel_masked, 1)
                lo = rel_rev[b * 64:(b + 1) * 64, :, :, 0:48].rearrange("p h j c -> p (h j) c")
                pool.affine_select(out=lo, in_=lo, compare_op=ALU.is_ge, fill=MASKED,
                                   base=8 - (GRID_W - 1), pattern=[[0, 6 * HEADS], [1, 48]],
                                   channel_multiplier=1).then_inc(rel_masked, 1)
            for b in range(2):
                pool.wait_ge(rel_masked, 2 + b)
                hi = rel_rev[b * 64:(b + 1) * 64, :, :, 16:64].rearrange("p h j c -> p (h j) c")
                pool.affine_select(out=hi, in_=hi, compare_op=ALU.is_ge, fill=MASKED,
                                   base=GRID_W - 1 + 7 - 16, pattern=[[0, 6 * HEADS], [-1, 48]],
                                   channel_multiplier=-1).then_inc(rel_masked, 1)
            pool.wait_ge(rel_masked, 4)
            pool.wait_ge(banks_free, evacuated(G_GATE - 1))
            with pool.Fori(0, HEADS) as h:
                pool.wait_ge(scores_ready, START + h * 3)
                for k in range(2):
                    pool.tensor_copy(stA[:, k, :], qkT[:, k, bass.ds(h, 1), :].rearrange("p a s -> p (a s)")
                                     ).then_inc(staged_qk, 1)
                pool.tensor_copy(stQb[:, :], qkT[:, 2, bass.ds(h, 1), :].rearrange("p a s -> p (a s)")
                                 ).then_inc(staged_qk, 1)
                pool.wait_ge(pv_done, START + h * 2)
                for k in range(2):
                    pool.tensor_copy(stV[:, k], vN[:, :, k, bass.ds(h * HEAD, HEAD)]
                                     ).then_inc(staged_v, 1)
            pool.wait_ge(staged_v, 2 * HEADS)
            pool.wait_ge(staged_qk, 3 * HEADS)
            pool.dma_start(res[:, :, :], x[0].rearrange("(t p) d -> p t d", p=P)).then_inc(res_loaded, 16)
            pool.wait_ge(oa_lo, START + HEADS)
            pool.dma_start(ln1_nat[:, 0, :], ln1_g[0].partition_broadcast(P)).then_inc(ln1_loaded, 16)
            pool.dma_start(ln1_nat[:, 1, :], ln1_b[0].partition_broadcast(P)).then_inc(ln1_loaded, 16)
            pool.wait_ge(ln1_loaded, 32)
            pool.wait_ge(x1t_turned, KC // 2)
            for t in range(TT):
                pool.tensor_tensor(res[:, t, :], res[:, t, :], ln1_nat[:, 0, :], ALU.mult
                                   ).then_inc(x1_nat, 1)
            for t in range(TT):
                pool.wait_ge(x1_nat, t + 1)
                pool.tensor_tensor(res[:, t, :], res[:, t, :], ln1_nat[:, 1, :], ALU.add
                                   ).then_inc(x1_nat, 1)
            pool.wait_ge(used, RING + N_DOWN)
            pool.dma_start(ln2_nat[:, 0, :], ln2_g[0].partition_broadcast(P)).then_inc(ln2_loaded, 16)
            pool.dma_start(ln2_nat[:, 1, :], ln2_b[0].partition_broadcast(P)).then_inc(ln2_loaded, 16)

        @block.tensor
        def _(pe):
            def three(acc, w, a, first, last):
                pe.matmul(acc, w[0], a[0], start=first, stop=False, skip_group_check=True)
                pe.matmul(acc, w[0], a[1], start=False, stop=False, skip_group_check=True)
                return pe.matmul(acc, w[1], a[0], start=False, stop=last, skip_group_check=True)

            def piece_feature_major(n, slot, j, count, bank, act_hi, act_lo):
                pe.wait_ge(residual, n + RING + 1)
                for a in range(PIECE_K):
                    k = j * PIECE_K + a
                    for s in range(SUB):
                        mm = three(ps[:, bank + s // 2, (s % 2) * SEQ:(s % 2 + 1) * SEQ],
                                   (w_hi[:, slot, a, s * P:(s + 1) * P], w_lo[:, slot, a, s * P:(s + 1) * P]),
                                   (act_hi[:, k, :], act_lo[:, k, :]),
                                   k == 0 and s % 2 == 0, k == count * PIECE_K - 1)
                mm.then_inc(used, 1)

            def piece_token_major(n, slot, j, count, bank, act_hi, act_lo):
                pe.wait_ge(residual, n + RING + 1)
                for a in range(PIECE_K):
                    k = j * PIECE_K + a
                    for t in range(TT):
                        acc = ps[:, bank + t, :]
                        hi, lo = act_hi[:, k, t * P:(t + 1) * P], act_lo[:, k, t * P:(t + 1) * P]
                        pe.matmul(acc, hi, w_hi[:, slot, a, :], start=(k == 0), stop=False)
                        pe.matmul(acc, hi, w_lo[:, slot, a, :], start=False, stop=False)
                        mm = pe.matmul(acc, lo, w_hi[:, slot, a, :], start=False,
                                       stop=(k == count * PIECE_K - 1))
                mm.then_inc(used, 1)

            def group(piece, n0, count, bank, act_hi, act_lo, slot0=0, between=None):
                for j in range(count):
                    if between:
                        between(j)
                    piece(n0 + j, (slot0 + j) % RING, j, count, bank, act_hi, act_lo)

            pe.sem_inc(used, RING)
            for s in (scores_ready, pv_done):
                pe.sem_inc(s, START)
            pe.wait_ge(ident_ready, 1)
            for b in range(KC // 2):
                if b % 2 == 0:
                    pe.wait_ge(x_loaded[b // 2], 16)
                for a in range(2):
                    for t in range(TT):
                        k = 2 * b + a
                        mm = pe.transpose(ps[:, b, a * SEQ + t * P:a * SEQ + (t + 1) * P],
                                          x_in[:, t, k * P:(k + 1) * P], ident[:, :])
                mm.then_inc(xt_ready, 1)
            pe.wait_ge(par_loaded, 16 * 7)
            pe.wait_ge(xt_lo, 4)
            for c, (r, col) in enumerate(((112, 0), (88, T_CW), (88, T_CW + 88), (88, T_CW + 176), (88, T_CB))):
                mm = pe.transpose(ps[:, 3, col:col + r], par[0:r, c, :], ident[0:r, 0:r])
            mm.then_inc(par_turned, 1)

            with pe.Fori(0, 4) as i:
                for u in range(2):
                    if u == 1:
                        pe.wait_ge(table_ready, 1)
                    pe.wait_ge(banks_free, G_QK + i * 2 + u + 1)
                    group(piece_feature_major, N_QK + i * 16 + u * PG, PG, 2 * u, xT_hi, xT_lo,
                          between=lambda j: pe.wait_ge(xt_lo, max(2, j + 1)))
            with pe.Fori(0, 2) as i:
                for u in range(2):
                    pe.wait_ge(banks_free, G_V + i * 2 + u + 1)
                    group(piece_token_major, N_V + i * 16 + u * PG, PG, 2 * u, xT_hi, xT_lo)

            def scores(h):
                pe.wait_ge(staged_qk, h * 3 + 3)
                pe.wait_ge(ob_lo, START + h)
                for m in range(2):
                    for t in range(TT):
                        mm = pe.matmul(ps[:, 4 + m, t * SEQ:(t + 1) * SEQ],
                                       stA[m * 64:(m + 1) * 64, 0, t * P:(t + 1) * P],
                                       stA[m * 64:(m + 1) * 64, 1, :], start=True, stop=True)
                    mm.then_inc(scores_ready, 1)
                for t in range(TT):
                    mm = pe.matmul(ps[:, 6, t * SEQ:(t + 1) * SEQ], stQb[:, t * P:(t + 1) * P],
                                   qkT[:, 3, bass.ds(h, 1), :].rearrange("p a s -> p (a s)"),
                                   start=True, stop=True)
                mm.then_inc(scores_ready, 1)

            def turn_probs(h):
                pe.wait_ge(normed_a, h + 1)
                for c in range(TT):
                    for t in range(TT):
                        mm = pe.transpose(ps[:, 7, c * SEQ + t * P:c * SEQ + (t + 1) * P],
                                          sA[:, 0, t, c * P:(c + 1) * P], ident[:, :])
                mm.then_inc(turned, 1)
                pe.wait_ge(normed_b, h + 1)
                for c in range(TT):
                    for t in range(TT):
                        mm = pe.transpose(ps[:, 6, c * SEQ + t * P:c * SEQ + (t + 1) * P],
                                          sB[:, t, c * P:(c + 1) * P], ident[:, :])
                mm.then_inc(turned, 1)

            def values(h):
                pe.wait_ge(staged_v, h * 2 + 2)
                for k, (probs, ready) in enumerate(((aT, aT_ready), (pT, pT_ready))):
                    pe.wait_ge(ready, h + 1)
                    for c in range(TT):
                        mm = pe.matmul(ps[:, 4 + 2 * k, 0:SEQ], stV[:, k, c, :], probs[:, c, :],
                                       start=(c == 0), stop=(c == TT - 1))
                    mm.then_inc(pv_done, 1)

            def mean_squares(h):
                pe.wait_ge(squared, h + 1)
                pe.matmul(ps[:, 7, 0:SEQ], ones[:, :], oa_sq, start=True, stop=True).then_inc(ms_ready, 1)

            pe.wait_ge(rel_masked, 4)
            pe.wait_ge(pool_steps, 4)
            rev = rel_rev[:, :, :, :].rearrange("p h j c -> p (h j c)")
            for r in range(6):
                if r >= 4:
                    pe.wait_ge(rel_copied, r - 3)
                pe.matmul(ps[:, 4 + r % 4, :], flip[:, :], rev[:, r * 512:(r + 1) * 512],
                          start=True, stop=True).then_inc(rel_flipped, 1)
            pe.wait_ge(rel_copied, 6)
            pe.wait_ge(const_ready, 1)
            with pe.Fori(0, 4) as i:
                for u in range(2):
                    h = i * 2 + u
                    steps = {0: scores, 4: turn_probs, 6: values, 7: mean_squares}
                    pe.wait_ge(banks_free, G_GATE + i * 2 + u + 1)
                    group(piece_feature_major, N_GATE + i * 16 + u * PG, PG, 2 * u, xT_hi, xT_lo,
                          between=lambda j: steps[j](h) if j in steps else None)

            pe.wait_ge(banks_free, evacuated(G_END - 2))
            pe.wait_ge(ob_lo, START + HEADS)
            with pe.Fori(0, 4) as c:
                pe.wait_ge(b_gated, START + c * 2)
                group(piece_feature_major, N_BRANCH + c * 8, PB, 0, obT_hi, obT_lo)
                pe.wait_ge(banks_free, evacuated(G_END - 1))
                pe.wait_ge(oa_lo, START + HEADS)
                pe.wait_ge(a_gated, START + c * 2)
                group(piece_feature_major, N_BRANCH + c * 8 + PB, PB, 2, oaT_hi, oaT_lo)
            pe.wait_ge(b_gated, START + 8)
            with pe.Fori(0, 2) as i:
                for u in range(2):
                    pe.wait_ge(res_steps, START + i * (2 + 2 * u))
                    group(piece_token_major, N_OUT + i * 16 + u * PG, PG, 2 * u, yT_hi, yT_lo,
                          between=lambda j: pe.wait_ge(y_lo, START + (8 if u else j + 1)))

            for b in range(KC // 2):
                if b % 2 == 0:
                    pe.wait_ge(xn0_ready, b // 2 + 1)
                    pe.wait_ge(xn1_ready, b // 2 + 1)
                for a in range(2):
                    for t in range(TT):
                        k = 2 * b + a
                        mm = pe.transpose(ps[:, b, a * SEQ + t * P:a * SEQ + (t + 1) * P],
                                          res[:, t, k * P:(k + 1) * P], ident[:, :])
                mm.then_inc(x1t_turned, 1)
            with pe.Fori(0, PAIRS_UP) as i:
                for u in range(2):
                    pe.wait_ge((g_conv, v_conv)[u], START + i * 2 * SUB)
                    group(piece_feature_major, N_UP + i * 16 + u * PG, PG, 2 * u, x1T_hi, x1T_lo,
                          between=lambda j: pe.wait_ge(x1_lo, max(2, j + 1)))
            with pe.Fori(0, 2) as i:
                for u in range(2):
                    pe.wait_ge((g_conv, v_conv)[u], START + PAIRS_UP * 2 * SUB)
                    pe.wait_ge(res_steps, START + i * (10 + 2 * u))
                    group(piece_token_major, N_DOWN + i * 2 * PF + u * PF, PF, 2 * u, hT_hi, hT_lo,
                          slot0=u * PF % RING,
                          between=lambda j: pe.wait_ge(h_lo, START + 2 * j + 2))

        @block.scalar
        def _(act):
            def round_piece(c, off4=0):
                slot = c % RING
                act.wait_ge(raw_loaded[slot], off4 * 16 + 16 * (c // RING + 1))
                act.wait_ge(used, off4 * RING + c + 1)
                act.activation(w_hi[:, slot], raw[:, slot], ACT.Copy).then_inc(rounded, 1)

            def rounds(c, count, off4=0, between=None):
                for j in range(count):
                    round_piece(c + j + LEAD, off4)
                    if between:
                        between(j)

            act.sem_inc(banks_free, 2)
            act.wait_ge(dist_raw, 1)
            act.activation(dist[:, :], dist[:, :], ACT.Abs).then_inc(dist_ready, 1)
            for b in range(KC // 2):
                act.wait_ge(xt_ready, b + 1)
                act.activation(xT_hi[:, 2 * b:2 * b + 2, :], ps[:, b, :].rearrange("p (a s) -> p a s", a=2),
                               ACT.Copy).then_inc(xt_hi, 1)
            act.wait_ge(par_turned, 1)
            act.activation(table[:, :], ps[:, 3, 0:T_ALL], ACT.Copy).then_inc(table_ready, 1)
            act.wait_ge(table_ready, 1)
            for c in range(LEAD):
                round_piece(c)
            act.wait_ge(lam_steps, 2)
            act.activation(lam_exp, lam_dot, ACT.Exp).then_inc(lam_exped, 1)

            def evacuate_columns(n_end, off4, g, bank, dst, dst0, col0):
                act.wait_ge(used, off4 * RING + RING + n_end)
                for s in range(SUB):
                    ev = act.activation(
                        dst[:, bass.ds(dst0 + s, 1), :].rearrange("p a s -> p (a s)"),
                        ps[:, bank + s // 2, (s % 2) * SEQ:(s % 2 + 1) * SEQ], ACT.Identity,
                        bias=table[:, bass.ds(col0 + s, 1)])
                ev.then_inc(banks_free, 1)

            qk_chunks = qkT[:, :, :, :].rearrange("p k h s -> p (k h) s")
            with act.Fori(0, 2) as a:
                with act.Fori(0, 2) as b:
                    for u in range(2):
                        off4 = a * 8 + b * 4
                        rounds(N_QK + u * PG, PG, off4)
                        evacuate_columns(N_QK + (u + 1) * PG, off4, None, 2 * u, qk_chunks,
                                         a * 16 + b * 8 + u * SUB, T_BIN + a * 24 + b * 8 + u * SUB)
            with act.Fori(0, 4) as i:
                rounds(N_V, PG, i * 2)

            def exponentials(h):
                act.wait_ge(maxed, h * 3 + 3)
                for m in range(2):
                    for t in range(TT):
                        k = m * TT + t
                        act.activation(sA[:, m, t, :], sA[:, m, t, :], ACT.Exp, scale=DIFF_SCALE,
                                       bias=neg_maxs[:, k:k + 1], accum_out=sums[:, k:k + 1]
                                       ).then_inc(exped, 1)
                for t in range(TT):
                    act.activation(sB[:, t, :], sB[:, t, :], ACT.Exp, bias=neg_max[:, 4 + t:5 + t],
                                   accum_out=sums[:, 4 + t:5 + t]).then_inc(exped, 1)

            def copy_pT(h):
                act.wait_ge(turned, h * 2 + 2)
                act.activation(pT[:, :, :], ps[:, 6, :].rearrange("p (c s) -> p c s", c=TT), ACT.Copy
                               ).then_inc(pT_ready, 1)

            def read_values(h):
                act.wait_ge(oa_copied, h + 1)
                act.activation(oa_sq, oa, ACT.Square).then_inc(squared, 1)
                act.wait_ge(pv_done, START + h * 2 + 2)
                act.activation(obT_hi[:, bass.ds(h, 1), :].rearrange("p a s -> p (a s)"),
                               ps[:, 6, 0:SEQ], ACT.Copy).then_inc(ob_hi, 1)

            def finish_a(h):
                act.wait_ge(ms_ready, h + 1)
                act.activation(oa_rms, ps[:, 7, 0:SEQ], ACT.Sqrt, bias=eps_c).then_inc(oa_sqrt, 1)
                act.wait_ge(oa_steps, h * 2 + 2)
                act.activation(oaT_hi[:, bass.ds(h, 1), :].rearrange("p a s -> p (a s)"), oa, ACT.Copy
                               ).then_inc(oa_hi, 1)

            act.wait_ge(banks_free, evacuated(G_GATE - 1))
            with act.Fori(0, 4) as i:
                for u in range(2):
                    h = i * 2 + u
                    steps = {1: exponentials, 4: copy_pT, 6: read_values, 7: finish_a}
                    rounds(N_GATE + u * PG, PG, i * 4,
                           between=lambda j: steps[j](h) if j in steps else None)
                    evacuate_columns(N_GATE + (u + 1) * PG, i * 4, None, 2 * u, gate,
                                     i * 8 + u * SUB, T_BIN + C_GATE // P + i * 8 + u * SUB)
            def gates_of(c):
                act.wait_ge(banks_free, evacuated(G_END - 1))
                for k in range(2):
                    part = gate[:, bass.ds(k * KC + c * SUB, SUB), :]
                    act.activation(part, part, ACT.Sigmoid).then_inc(gates_on, 1)

            def high_y(c, j):
                if j == 1:
                    for pair in range(2):
                        act.wait_ge(y_summed, c * 2 + 1 + pair)
                        chunk = c * SUB + 2 * pair
                        act.activation(yT_hi[:, bass.ds(chunk, 2), :], gate[:, bass.ds(chunk, 2), :],
                                       ACT.Copy).then_inc(y_hi, 1)

            rounds(N_BRANCH, PB, between=lambda j: gates_of(0) if j == 2 else None)
            with act.Fori(0, 3) as c:
                rounds(N_BRANCH + PB, PB, c * 2)
                rounds(N_BRANCH + 2 * PB, PB, c * 2,
                       between=lambda j: gates_of(c + 1) if j == 2 else high_y(c, j))
            rounds(N_OUT - PB, PB)
            rounds(N_OUT, PG, between=lambda j: high_y(3, j))
            with act.Fori(0, 3) as i:
                rounds(N_OUT + PG, PG, i * 2)
            act.wait_ge(ln_steps, 3)
            act.activation(std, vpe, ACT.Sqrt).then_inc(ln_sqrt, 1)
            act.wait_ge(ln_steps, 5)
            for q in range(4):
                part = res[:, 1, q * 512:(q + 1) * 512]
                act.activation(part, part, ACT.Identity, scale=rstd[:, 1:2], bias=shift[:, 1:2]
                               ).then_inc(xn1_ready, 1)
            for b in range(KC // 2):
                act.wait_ge(x1_aff, 2 * b + 2)
                act.activation(x1T_hi[:, 2 * b:2 * b + 2, :],
                               x1f[:, b % 4, :].rearrange("p (a s) -> p a s", a=2), ACT.Copy
                               ).then_inc(x1_hi, 1)

            def mid(i, s, dst, bank, first, done):
                act.activation(dst[:, s, :], ps[:, bank + s // 2, (s % 2) * SEQ:(s % 2 + 1) * SEQ],
                               ACT.Identity, bias=table[:, bass.ds(T_CB + first + i * SUB + s, 1)],
                               scale=table[:, bass.ds(T_CW + 88 + first + i * SUB + s, 1)]
                               ).then_inc(done, 1)

            def gate_steps(i, j):
                if j == 0:
                    act.wait_ge(used, i * 16 + RING + N_UP + PG)
                    act.wait_ge(h_lo, START + i * SUB)
                if j in (0, 1):
                    for s in (2 * j, 2 * j + 1):
                        mid(i, s, cg, 0, 0, g_mid)
                if j in (3, 4):
                    for s in (2 * j - 6, 2 * j - 5):
                        act.wait_ge(g_conv, START + i * 2 * SUB + 4 * (j - 2))
                        act.activation(cg[:, s, :], cg[:, s, :], ACT.Gelu).then_inc(g_act, 1)

            def value_steps(i, j):
                if j == 0:
                    act.wait_ge(used, i * 16 + RING + N_UP + 2 * PG)
                    act.wait_ge(h_ready, START + i * SUB)
                if j in (0, 1):
                    for s in (2 * j, 2 * j + 1):
                        mid(i, s, cv, 2, FC, v_mid)
                if j in (4, 5):
                    for s in (2 * j - 8, 2 * j - 7):
                        act.wait_ge(h_ready, START + i * SUB + s + 1)
                        act.activation(hT_hi[:, bass.ds(i * SUB + s, 1), :].rearrange("p a s -> p (a s)"),
                                       cg[:, s, :], ACT.Copy).then_inc(h_hi, 1)

            rounds(N_UP, PG)
            last = PAIRS_UP - 1
            with act.Fori(0, last) as i:
                rounds(N_UP + PG, PG, i * 4, between=lambda j: gate_steps(i, j))
                rounds(N_UP + 2 * PG, PG, i * 4, between=lambda j: value_steps(i, j))
            rounds(N_UP + PG, PG, last * 4, between=lambda j: gate_steps(last, j))
            rounds(N_DOWN, PG, 0, between=lambda j: value_steps(last, j))
            with act.Fori(0, 9) as i:
                rounds(N_DOWN + PG, 8, i * 2)
            rounds(N_DOWN + PG + 72, 88 - PG - 72 - LEAD)
            act.wait_ge(ln_steps, 8)
            act.activation(std, vpe, ACT.Sqrt).then_inc(ln_sqrt, 1)

        @block.vector
        def _(dve):
            def split_piece(c, off4=0):
                slot = c % RING
                dve.wait_ge(rounded, off4 * RING + c + 1)
                dve.tensor_tensor(w_lo[:, slot], raw[:, slot], w_hi[:, slot].bitcast(F32), ALU.subtract
                                  ).then_inc(residual, 1)

            def splits(c, count, off4=0, between=None, before=None):
                for j in range(count):
                    if before:
                        before(j)
                    split_piece(c + j + LEAD, off4)
                    if between:
                        between(j)

            dve.sem_inc(residual, RING)
            for s in (ob_lo, oa_lo, b_gated, a_gated, y_lo, res_steps, g_conv, v_conv, h_ready, h_lo):
                dve.sem_inc(s, START)
            for h in range(HEADS):
                dve.memset(slope8[:, h:h + 1], -(2.0 ** -(h + 1)) / DIFF_SCALE).then_inc(consts_set, 1)
            dve.memset(eps_c, RMS_EPS).then_inc(consts_set, 1)
            for b in range(KC // 2):
                dve.wait_ge(xt_hi, b + 1)
                dve.tensor_tensor(xT_lo[:, 2 * b:2 * b + 2, :],
                                  ps[:, b, :].rearrange("p (a s) -> p a s", a=2),
                                  xT_hi[:, 2 * b:2 * b + 2, :].bitcast(F32), ALU.subtract
                                  ).then_inc(xt_lo, 1)
            for c in range(LEAD):
                split_piece(c)
            dve.wait_ge(lam_loaded, 16 * 5)
            dve.tensor_tensor(lamv[:, 0:2, :], lamv[:, 0:2, :], lamv[:, 2:4, :], ALU.mult
                              ).then_inc(lam_steps, 1)
            dve.wait_ge(lam_steps, 1)
            dve.tensor_reduce(lam_dot, lamv[:, 0:2, :], AX.X, ALU.add).then_inc(lam_steps, 1)
            dve.tensor_scalar(subg8, subg, 1.0 - LAMBDA_INIT, None, ALU.mult).then_inc(lam_steps, 1)
            dve.wait_ge(lam_exped, 1)
            dve.tensor_tensor(lam_dif, lam_exp[:, 1:2], lam_exp[:, 0:1], ALU.subtract
                              ).then_inc(lam_steps, 1)
            dve.wait_ge(lam_steps, 4)
            dve.tensor_scalar(neg_lam, lam_dif, -LAMBDA_INIT, None, ALU.add).then_inc(lam_steps, 1)
            with dve.Fori(0, 8) as i:
                splits(N_QK, PG, i * 2)
            dve.wait_ge(vbias_loaded, 32)
            dve.wait_ge(banks_free, evacuated(G_V - 1))
            with dve.Fori(0, 2) as i:
                for u in range(2):
                    splits(N_V + u * PG, PG, i * 4)
                    dve.wait_ge(used, i * 16 + RING + N_V + (u + 1) * PG)
                    for t in range(TT):
                        ev = dve.tensor_tensor(
                            vN[:, t, bass.ds(i, 1), u * GROUP:(u + 1) * GROUP].rearrange("p a n -> p (a n)"),
                            ps[:, 2 * u + t, :],
                            vbias[:, bass.ds(i, 1), u * GROUP:(u + 1) * GROUP].rearrange("p a n -> p (a n)"),
                            ALU.add)
                    ev.then_inc(banks_free, 1)

            def bias_and_max(h):
                dve.wait_ge(oa_lo, START + h)
                for m in range(2):
                    dve.wait_ge(scores_ready, START + h * 3 + m + 1)
                    for t in range(TT):
                        dve.scalar_tensor_tensor(
                            sA[:, m, t, :], dist[:, P - t * P:P - t * P + SEQ], slope8[:, bass.ds(h, 1)],
                            ps[:, 4 + m, t * SEQ:(t + 1) * SEQ], ALU.mult, ALU.add).then_inc(biased, 1)
                dve.wait_ge(scores_ready, START + h * 3 + 3)
                for t in range(TT):
                    dve.scalar_tensor_tensor(
                        sB[:, t, :], ps[:, 6, t * SEQ:(t + 1) * SEQ], NA_SCALE,
                        rel[:, bass.ds(h, 1), 2 - 2 * t:6 - 2 * t, :].rearrange("p a j c -> p (a j c)"),
                        ALU.mult, ALU.add).then_inc(biased, 1)
                dve.wait_ge(biased, h * 6 + 4)
                dve.tensor_reduce(neg_max[:, 0:4], sA[:, :, :, :].rearrange("p m t s -> p (m t) s"), AX.X,
                                  ALU.max, negate=True).then_inc(maxed, 1)
                dve.wait_ge(biased, h * 6 + 6)
                dve.tensor_reduce(neg_max[:, 4:6], sB[:, :, :], AX.X, ALU.max, negate=True
                                  ).then_inc(maxed, 1)
                dve.wait_ge(maxed, h * 3 + 1)
                dve.tensor_scalar(neg_maxs, neg_max[:, 0:4], DIFF_SCALE, None, ALU.mult
                                  ).then_inc(maxed, 1)

            def normalise(h):
                dve.wait_ge(exped, h * 6 + 6)
                dve.reciprocal(rsum, sums).then_inc(soft, 1)
                dve.wait_ge(soft, h * 4 + 1)
                dve.tensor_scalar(coef, rsum[:, 2:4], neg_lam, None, ALU.mult).then_inc(soft, 1)
                for t in range(TT):
                    dve.tensor_scalar(sA[:, 0, t, :], sA[:, 0, t, :], rsum[:, t:t + 1], None, ALU.mult
                                      ).then_inc(soft, 1)
                for t in range(TT):
                    op = dve.tensor_scalar(sB[:, t, :], sB[:, t, :], rsum[:, 4 + t:5 + t], None, ALU.mult)
                op.then_inc(normed_b, 1)
                dve.wait_ge(soft, h * 4 + 4)
                for t in range(TT):
                    op = dve.scalar_tensor_tensor(sA[:, 0, t, :], sA[:, 1, t, :], coef[:, t:t + 1],
                                                  sA[:, 0, t, :], ALU.mult, ALU.add)
                op.then_inc(normed_a, 1)

            def copy_aT(h):
                dve.wait_ge(turned, h * 2 + 1)
                dve.tensor_copy(aT[:, :, :], ps[:, 7, :].rearrange("p (c s) -> p c s", c=TT)
                                ).then_inc(aT_ready, 1)

            def read_values(h):
                dve.wait_ge(pv_done, START + h * 2 + 1)
                dve.tensor_copy(oa, ps[:, 4, 0:SEQ]).then_inc(oa_copied, 1)
                dve.wait_ge(ob_hi, h + 1)
                dve.tensor_tensor(obT_lo[:, bass.ds(h, 1), :].rearrange("p a s -> p (a s)"),
                                  ps[:, 6, 0:SEQ],
                                  obT_hi[:, bass.ds(h, 1), :].bitcast(F32).rearrange("p a s -> p (a s)"),
                                  ALU.subtract).then_inc(ob_lo, 1)

            def finish_a(h):
                dve.wait_ge(oa_sqrt, h + 1)
                dve.reciprocal(oa_rms, oa_rms).then_inc(oa_steps, 1)
                dve.wait_ge(oa_steps, h * 2 + 1)
                dve.scalar_tensor_tensor(oa, oa, subg8, oa_rms, ALU.mult, ALU.mult).then_inc(oa_steps, 1)
                dve.wait_ge(oa_hi, h + 1)
                dve.tensor_tensor(oaT_lo[:, bass.ds(h, 1), :].rearrange("p a s -> p (a s)"), oa,
                                  oaT_hi[:, bass.ds(h, 1), :].bitcast(F32).rearrange("p a s -> p (a s)"),
                                  ALU.subtract).then_inc(oa_lo, 1)

            dve.wait_ge(dist_ready, 1)
            for r in range(6):
                dve.wait_ge(rel_flipped, r + 1)
                dve.tensor_copy(rel[:, :, :, :].rearrange("p h j c -> p (h j c)")[:, r * 512:(r + 1) * 512],
                                ps[:, 4 + r % 4, :]).then_inc(rel_copied, 1)
            dve.wait_ge(rel_copied, 6)
            dve.wait_ge(consts_set, HEADS + 1)
            dve.wait_ge(lam_steps, 5)
            with dve.Fori(0, 4) as i:
                for u in range(2):
                    h = i * 2 + u
                    steps = {1: normalise, 4: copy_aT, 6: read_values, 7: finish_a}
                    splits(N_GATE + u * PG, PG, i * 4,
                           before=lambda j: bias_and_max(h) if j == 0 else None,
                           between=lambda j: steps[j](h) if j in steps else None)
            def gated(c, k, pair):
                chunk = k * KC + c * SUB + 2 * pair
                dve.tensor_tensor(gate[:, bass.ds(chunk, 2), :],
                                  ps[:, 2 - 2 * k + pair, :].rearrange("p (a s) -> p a s", a=2),
                                  gate[:, bass.ds(chunk, 2), :], ALU.mult
                                  ).then_inc(b_gated if k else a_gated, 1)

            def gate_b(c, j):
                if j == 0:
                    dve.wait_ge(gates_on, c * 2 + 2)
                    dve.wait_ge(used, c * 8 + RING + N_BRANCH + PB)
                    for pair in range(2):
                        gated(c, 1, pair)

            def sum_branches(c, j):
                if j == 0:
                    dve.wait_ge(used, c * 8 + RING + N_BRANCH + 2 * PB)
                    for pair in range(2):
                        gated(c, 0, pair)
                    for pair in range(2):
                        dve.wait_ge(b_gated, START + c * 2 + pair + 1)
                        dve.wait_ge(a_gated, START + c * 2 + pair + 1)
                        chunk = c * SUB + 2 * pair
                        dve.tensor_tensor(gate[:, bass.ds(chunk, 2), :], gate[:, bass.ds(chunk, 2), :],
                                          gate[:, bass.ds(chunk + KC, 2), :], ALU.add
                                          ).then_inc(y_summed, 1)
                if j == 1:
                    for pair in range(2):
                        chunk = c * SUB + 2 * pair
                        dve.wait_ge(y_hi, c * 2 + pair + 1)
                        dve.tensor_tensor(yT_lo[:, bass.ds(chunk, 2), :], gate[:, bass.ds(chunk, 2), :],
                                          yT_hi[:, bass.ds(chunk, 2), :].bitcast(F32), ALU.subtract
                                          ).then_inc(y_lo, 1)

            splits(N_BRANCH, PB)
            with dve.Fori(0, 3) as c:
                splits(N_BRANCH + PB, PB, c * 2, between=lambda j: gate_b(c, j))
                splits(N_BRANCH + 2 * PB, PB, c * 2, between=lambda j: sum_branches(c, j))
            splits(N_OUT - PB, PB, between=lambda j: gate_b(3, j))

            def read_out(q, bank, n_end, steps0):
                dve.wait_ge(used, RING + n_end)
                for t in range(TT):
                    part = res[:, t, bass.ds(q * GROUP, GROUP)]
                    dve.scalar_tensor_tensor(part, part, ALPHA, ps[:, bank + t, :], ALU.mult, ALU.add
                                             ).then_inc(res_steps, 1)
                for t in range(TT):
                    dve.wait_ge(res_steps, START + steps0 + t + 1)
                    dve.bn_stats(stats[:, t, bass.ds(q, 1), :].rearrange("p a s -> p (a s)"),
                                 res[:, t, bass.ds(q * GROUP, GROUP)]).then_inc(stat_steps, 1)

            def statistics(k):
                for t in range(TT):
                    dve.wait_ge(stat_steps, 8 * (k + 1))
                    dve.bn_aggr(mv[:, t, :], stats[:, t, :, :].rearrange("p g s -> p (g s)")
                                ).then_inc(ln_steps, 1)
                dve.wait_ge(ln_steps, 5 * k + 2)
                dve.tensor_scalar(vpe, mv[:, :, 1:2].rearrange("p t a -> p (t a)"), LN_EPS, None, ALU.add
                                  ).then_inc(ln_steps, 1)
                dve.wait_ge(ln_sqrt, k + 1)
                dve.reciprocal(rstd, std).then_inc(ln_steps, 1)
                dve.wait_ge(ln_steps, 5 * k + 4)

            dve.wait_ge(res_loaded, 16)
            splits(N_OUT, PG, between=lambda j: sum_branches(3, j))
            read_out(0, 0, N_OUT + PG, 0)
            for q in range(1, 4):
                splits(N_OUT + q * PG, PG)
                read_out(q, 2 * (q % 2), N_OUT + (q + 1) * PG, q * 2)
            statistics(0)
            dve.scalar_tensor_tensor(shift, mv[:, :, 0:1].rearrange("p t a -> p (t a)"), -1.0, rstd,
                                     ALU.mult, ALU.mult).then_inc(ln_steps, 1)
            for q in range(4):
                part = res[:, 0, q * 512:(q + 1) * 512]
                dve.tensor_scalar(part, part, mv[:, 0, 0:1], rstd[:, 0:1], ALU.subtract, ALU.mult
                                  ).then_inc(xn0_ready, 1)

            def affine(b):
                dve.wait_ge(x1t_turned, b + 1)
                if b >= 4:
                    dve.wait_ge(x1_lo, b - 3)
                for a in range(2):
                    k = 2 * b + a
                    dve.tensor_scalar(x1f[:, b % 4, a * SEQ:(a + 1) * SEQ], ps[:, b, a * SEQ:(a + 1) * SEQ],
                                      table[:, T_LNG + k:T_LNG + k + 1], table[:, T_LNB + k:T_LNB + k + 1],
                                      ALU.mult, ALU.add).then_inc(x1_aff, 1)

            def low_x1(b):
                dve.wait_ge(x1_hi, b + 1)
                dve.tensor_tensor(x1T_lo[:, 2 * b:2 * b + 2, :],
                                  x1f[:, b % 4, :].rearrange("p (a s) -> p a s", a=2),
                                  x1T_hi[:, 2 * b:2 * b + 2, :].bitcast(F32), ALU.subtract
                                  ).then_inc(x1_lo, 1)

            affine(0)
            for b in range(1, KC // 2):
                affine(b)
                low_x1(b - 1)
            low_x1(KC // 2 - 1)

            def taps(i, j, dst, bank, first, mids, done):
                s0, count = 2 * (j - 1), i * 2 * SUB + 4 * (j - 1)
                dve.wait_ge(mids, i * SUB + s0 + 2)
                for s in (s0, s0 + 1):
                    dve.scalar_tensor_tensor(
                        dst[:, s, 1:SEQ], ps[:, bank + s // 2, (s % 2) * SEQ:(s % 2 + 1) * SEQ - 1],
                        table[:, bass.ds(T_CW + first + i * SUB + s, 1)], dst[:, s, 1:SEQ],
                        ALU.mult, ALU.add).then_inc(done, 1)
                for s in (s0, s0 + 1):
                    dve.wait_ge(done, START + count + s - s0 + 1)
                    dve.scalar_tensor_tensor(
                        dst[:, s, 0:SEQ - 1], ps[:, bank + s // 2, (s % 2) * SEQ + 1:(s % 2 + 1) * SEQ],
                        table[:, bass.ds(T_CW + 176 + first + i * SUB + s, 1)], dst[:, s, 0:SEQ - 1],
                        ALU.mult, ALU.add).then_inc(done, 1)

            def gate_steps(i, j):
                if j in (1, 2):
                    taps(i, j, cg, 0, 0, g_mid, g_conv)

            def value_steps(i, j):
                if j in (1, 2):
                    taps(i, j, cv, 2, FC, v_mid, v_conv)
                if j == 3:
                    dve.wait_ge(v_conv, START + i * 2 * SUB + 2 * SUB)
                    dve.wait_ge(g_act, i * SUB + SUB)
                    for s in range(SUB):
                        dve.tensor_tensor(cg[:, s, :], cg[:, s, :], cv[:, s, :], ALU.mult
                                          ).then_inc(h_ready, 1)
                if j in (5, 6):
                    for s in (2 * j - 10, 2 * j - 9):
                        chunk = bass.ds(i * SUB + s, 1)
                        dve.wait_ge(h_hi, i * SUB + s + 1)
                        dve.tensor_tensor(hT_lo[:, chunk, :].rearrange("p a s -> p (a s)"), cg[:, s, :],
                                          hT_hi[:, chunk, :].bitcast(F32).rearrange("p a s -> p (a s)"),
                                          ALU.subtract).then_inc(h_lo, 1)

            splits(N_UP, PG)
            last = PAIRS_UP - 1
            dve.wait_ge(x1_nat, 2 * TT)
            with dve.Fori(0, last) as i:
                splits(N_UP + PG, PG, i * 4, between=lambda j: gate_steps(i, j))
                splits(N_UP + 2 * PG, PG, i * 4, between=lambda j: value_steps(i, j))
            splits(N_UP + PG, PG, last * 4, between=lambda j: gate_steps(last, j))
            for q in range(4):
                splits(N_DOWN + q * PF, PF if q < 3 else PF - LEAD, 0,
                       between=(lambda j: value_steps(last, j)) if q == 0 else None)
                read_out(q, 2 * (q % 2), N_DOWN + (q + 1) * PF, 8 + q * 2)
            statistics(1)
            dve.wait_ge(ln2_loaded, 32)
            blocks = [(t, q) for t in range(TT) for q in range(4)]

            def centre(t, q):
                part = res[:, t, q * 512:(q + 1) * 512]
                dve.scalar_tensor_tensor(part, part, mv[:, t, 0:1], ln2_nat[:, 0, q * 512:(q + 1) * 512],
                                         ALU.subtract, ALU.mult).then_inc(out_steps, 1)

            def scale(n, t, q):
                part = res[:, t, q * 512:(q + 1) * 512]
                dve.wait_ge(out_steps, n + 1)
                dve.scalar_tensor_tensor(part, part, rstd[:, t:t + 1], ln2_nat[:, 1, q * 512:(q + 1) * 512],
                                         ALU.mult, ALU.add).then_inc(out_ready, 1)

            centre(*blocks[0])
            for n in range(1, len(blocks)):
                centre(*blocks[n])
                scale(n - 1, *blocks[n - 1])
            scale(len(blocks) - 1, *blocks[-1])


_INS = ["x", "w_in", "b_in", "lam_q1", "lam_k1", "lam_q2", "lam_k2", "subln_g", "rpb", "w_branch_a",
        "w_branch_b", "w_out", "ln1_g", "ln1_b", "w_up", "conv_w", "conv_b", "w_down", "ln2_g", "ln2_b"]


def kernel(**inputs):
    import numpy as _np
    import concourse.bacc as _bacc
    from concourse import mybir as _mybir
    from concourse.bass_utils import run_bass_kernel_spmd as _run

    nc = _bacc.Bacc("TRN2", target_bir_lowering=False, num_devices=1)
    arrays, args = {}, []
    for name in _INS:
        a = _np.ascontiguousarray(inputs[name])
        arrays[f"in_{name}"] = a
        args.append(nc.dram_tensor(f"in_{name}", a.shape, _mybir.dt.from_np(a.dtype), kind="ExternalInput").ap())
    args.append(nc.dram_tensor("out_0", (1, SEQ, D_MODEL), F32, kind="ExternalOutput").ap())
    encoder_block(nc, *args)
    r = _run(nc, [arrays], core_ids=[0])
    return r.results[0]["out_0"]
```

```python
import math
from contextlib import ExitStack

import concourse.bass as bass
from concourse import mybir
from concourse.alu_op_type import AluOpType as ALU

ACT = mybir.ActivationFunctionType
AX = mybir.AxisListType
F32 = mybir.dt.float32
F32R = mybir.dt.float32r

P = 128
D_MODEL = 2048
SEQ = 256
TT = SEQ // P
KC = D_MODEL // P
HEADS = 8
QK_DIM = 64
HEAD = 128
WIDTH = HEADS * HEAD
GRID_W = 64
NA_KC = 16
RPB_R, RPB_C = 15, 31
D_FF = 5632
FC = D_FF // P
LN_EPS = 1e-5
RMS_EPS = 1e-5
ALPHA = 2.0 ** 0.25
LAMBDA_INIT = 0.8 - 0.6 * math.exp(0.0)
DIFF_SCALE = QK_DIM ** -0.5
NA_SCALE = HEAD ** -0.5
MASKED = -1.0e30

GROUP = 512
SUB = GROUP // P
PIECE_K = 2
RING = 4
START = 1
LEAD = RING - 1

PG = KC // PIECE_K
PB = WIDTH // P // PIECE_K
PF = FC // PIECE_K
G_QK, G_V, G_GATE = 0, 8, 12
G_END = 20
N_QK, N_V, N_GATE = 0, 64, 96
N_BRANCH, N_OUT, N_UP, N_DOWN, N_ALL = 160, 192, 224, 400, 488
PAIRS_UP = D_FF // GROUP

BLOCKS_SHARED = [(0, 0), (0, 1), (0, 2)]
BLOCKS_VECTOR = [(0, 3), (1, 0), (1, 1), (1, 2), (1, 3)]

C_QA, C_VA, C_QB, C_VB, C_GATE = 0, 2048, 3072, 5120, 6144
T_BIN, T_LNG, T_LNB, T_CW, T_CB, T_ALL = 0, 80, 96, 112, 376, 464


def encoder_block(nc, x, w_in, b_in, lam_q1, lam_k1, lam_q2, lam_k2, subln_g, rpb, w_branch_a,
                  w_branch_b, w_out, ln1_g, ln1_b, w_up, conv_w, conv_b, w_down, ln2_g, ln2_b, out):
    ctx = ExitStack()
    with ctx:
        base = (nc.sbuf_base + 31) // 32 * 32

        def at(name, offset, shape, dtype=F32):
            return nc.alloc_sbuf_tensor_at(name, shape, dtype, offset=base + offset)

        def sem(name):
            return ctx.enter_context(nc.semaphore(name))

        piece_bytes = PIECE_K * GROUP * 4
        o = 0
        raw = at("raw", o, [P, RING, PIECE_K, GROUP]); o += RING * piece_bytes
        w_hi = at("w_hi", o, [P, RING, PIECE_K, GROUP], F32R); o += RING * piece_bytes
        w_lo = at("w_lo", o, [P, RING, PIECE_K, GROUP], F32R); o += RING * piece_bytes
        ident = at("ident", o, [P, P]); o += P * 4
        table = at("table", o, [P, T_ALL]); o += T_ALL * 4
        small = at("small", o, [P, 120]); o += 480
        r1 = o
        xT_hi = at("xT_hi", o, [P, KC, SEQ], F32R)
        xT_lo = at("xT_lo", o + 16384, [P, KC, SEQ], F32R)
        yT_hi = at("yT_hi", o, [P, KC, SEQ], F32R)
        yT_lo = at("yT_lo", o + 16384, [P, KC, SEQ], F32R)
        o += 32768
        qkT = at("qkT", o, [P, 4, HEADS, SEQ])
        obT_hi = at("obT_hi", o + 16384, [P, HEADS, SEQ], F32R)
        obT_lo = at("obT_lo", o + 24576, [P, HEADS, SEQ], F32R)
        o += 32768
        rel = at("rel", o, [P, HEADS, 6, GRID_W]); o += 12288
        dist = at("dist", o, [P, 384]); o += 1536
        ones = at("ones", o, [P, P]); o += 512
        sA = at("sA", o, [P, 2, TT, SEQ]); o += 4096
        sB = at("sB", o, [P, TT, SEQ]); o += 2048
        aT = at("aT", o, [P, TT, SEQ]); o += 2048
        pT = at("pT", o, [P, TT, SEQ]); o += 2048
        hT_hi = at("hT_hi", r1, [P, FC, SEQ], F32R)
        hT_lo = at("hT_lo", r1 + FC * SEQ * 4, [P, FC, SEQ], F32R)
        assert o - r1 == 2 * FC * SEQ * 4
        ln1_nat = at("ln1_nat", r1 + (2 * FC - 16) * SEQ * 4, [P, 2, D_MODEL])
        r2 = o
        gate = at("gate", r2, [P, 2 * KC, SEQ])
        x_in = at("x_in", r2, [P, TT, D_MODEL])
        vbias = at("vbias", r2 + 16384, [P, 2, WIDTH])
        x1T_hi = at("x1T_hi", r2, [P, KC, SEQ], F32R)
        x1T_lo = at("x1T_lo", r2 + 16384, [P, KC, SEQ], F32R)
        ln2_nat = at("ln2_nat", r2, [P, 2, D_MODEL])
        o += 32768
        vN = at("vN", o, [P, TT, 2, WIDTH])
        res = at("res", o, [P, TT, D_MODEL])
        o += 16384
        r4 = o
        par = at("par", r4, [P, 5, P])
        lamv = at("lamv", r4 + 2560, [P, 4, QK_DIM])
        oaT_hi = at("oaT_hi", r4, [P, HEADS, SEQ], F32R)
        oaT_lo = at("oaT_lo", r4 + 8192, [P, HEADS, SEQ], F32R)
        x1f = at("x1f", r4, [P, 4, PIECE_K * SEQ])
        cg = at("cg", r4 + 8192, [P, SUB, SEQ])
        cv = at("cv", r4 + 12288, [P, SUB, SEQ])
        o += 16384
        stA = at("stA", o, [P, 2, SEQ])
        stQb = at("stQb", o + 2048, [P, SEQ])
        stV = at("stV", o + 3072, [P, 2, TT, HEAD])
        o += 5120
        assert base + o <= nc.sbuf_usable_end

        slope8 = small[:, 0:8]
        neg_max = small[:, 8:14]
        neg_maxs = small[:, 14:18]
        sums = small[:, 18:24]
        rsum = small[:, 24:30]
        coef = small[:, 30:32]
        lam_dot = small[:, 32:34]
        lam_exp = small[:, 34:36]
        lam_dif = small[:, 36:37]
        neg_lam = small[:, 37:38]
        subg = small[:, 38:39]
        subg8 = small[:, 39:40]
        stats = small[:, 40:88].rearrange("p (t g s) -> p t g s", t=TT, g=4)
        mv = small[:, 88:92].rearrange("p (t s) -> p t s", t=TT)
        std = small[:, 92:94]
        rstd = small[:, 94:96]
        eps_c = small[:, 96:97]
        oa = sB[:, 0, :]
        oa_rms = sA[:, 1, 1, :]
        oa_sq = sA[:, 1, 0, :]
        vpe = small[:, 98:100]
        shift = small[:, 100:102]

        ps = ctx.enter_context(nc.psum_tensor("ps", [P, 8, 512], F32))

        raw_loaded = [sem(f"raw_loaded{s}") for s in range(RING)]
        rounded = sem("rounded")
        residual = sem("residual")
        used = sem("used")
        banks_free = sem("banks_free")
        x_loaded = [sem(f"x_loaded{q}") for q in range(4)]
        ident_ready = sem("ident_ready")
        ones_ready = sem("ones_ready")
        consts_set = sem("consts_set")
        pool_steps = sem("pool_steps")
        par_loaded = sem("par_loaded")
        rel_loaded = sem("rel_loaded")
        rel_masked = sem("rel_masked")
        vbias_loaded = sem("vbias_loaded")
        lam_loaded = sem("lam_loaded")
        xt_ready = sem("xt_ready")
        xt_hi = sem("xt_hi")
        xt_lo = sem("xt_lo")
        par_turned = sem("par_turned")
        table_ready = sem("table_ready")
        dist_raw = sem("dist_raw")
        dist_ready = sem("dist_ready")
        lam_steps = sem("lam_steps")
        lam_exped = sem("lam_exped")
        staged_qk = sem("staged_qk")
        staged_v = sem("staged_v")
        scores_ready = sem("scores_ready")
        biased = sem("biased")
        maxed = sem("maxed")
        exped = sem("exped")
        soft = sem("soft")
        normed_a = sem("normed_a")
        normed_b = sem("normed_b")
        turned = sem("turned")
        aT_ready = sem("aT_ready")
        pT_ready = sem("pT_ready")
        pv_done = sem("pv_done")
        oa_copied = sem("oa_copied")
        squared = sem("squared")
        ms_ready = sem("ms_ready")
        ob_hi = sem("ob_hi")
        ob_lo = sem("ob_lo")
        oa_sqrt = sem("oa_sqrt")
        oa_steps = sem("oa_steps")
        oa_hi = sem("oa_hi")
        oa_lo = sem("oa_lo")
        gates_on = sem("gates_on")
        b_gated = sem("b_gated")
        a_gated = sem("a_gated")
        y_summed = sem("y_summed")
        y_hi = sem("y_hi")
        y_lo = sem("y_lo")
        res_loaded = sem("res_loaded")
        ln1_loaded = sem("ln1_loaded")
        ln2_loaded = sem("ln2_loaded")
        res_steps = sem("res_steps")
        stat_steps = sem("stat_steps")
        ln_steps = sem("ln_steps")
        ln_sqrt = sem("ln_sqrt")
        tile0_sums = sem("tile0_sums")
        xn0_ready = sem("xn0_ready")
        xn1_ready = sem("xn1_ready")
        xn1_rest_ready = sem("xn1_rest_ready")
        shared_normed = sem("shared_normed")
        shared_steps = sem("shared_steps")
        x1t_turned = sem("x1t_turned")
        x1_aff = sem("x1_aff")
        x1_aff2 = sem("x1_aff2")
        x1_hi = sem("x1_hi")
        x1_lo = sem("x1_lo")
        x1_nat = sem("x1_nat")
        g_mid = sem("g_mid")
        g_conv = sem("g_conv")
        g_act = sem("g_act")
        v_mid = sem("v_mid")
        v_conv = sem("v_conv")
        h_ready = sem("h_ready")
        h_hi = sem("h_hi")
        h_lo = sem("h_lo")
        out_ready = sem("out_ready")
        out_steps = sem("out_steps")
        out_stored = sem("out_stored")

        block = ctx.enter_context(nc.Block())

        def evacuated(g):
            return g + 3

        def pieces(weights):
            return weights.rearrange("(j a p) n -> j p a n", a=PIECE_K, p=P)

        w_in_p, w_a_p, w_b_p = pieces(w_in[0]), pieces(w_branch_a[0]), pieces(w_branch_b[0])
        w_out_p, w_up_p, w_down_p = pieces(w_out[0]), pieces(w_up[0]), pieces(w_down[0])

        @block.sync
        def _(sp):
            def load_x(q):
                sp.dma_start(x_in[:, :, q * 512:(q + 1) * 512],
                             x[0].rearrange("(t p) d -> p t d", p=P)[:, :, q * 512:(q + 1) * 512]
                             ).then_inc(x_loaded[q], 16)

            def load_group(src, count, n0, col, slot0=0, first=0):
                for j in range(first, count):
                    slot = (slot0 + j) % RING
                    sp.wait_ge(residual, n0 + j + 1)
                    sp.dma_start(raw[:, slot], src[j][:, :, bass.ds(col, GROUP)]
                                 ).then_inc(raw_loaded[slot], 16)

            load_x(0)
            for j in range(LEAD):
                load_group(w_in_p, j + 1, N_QK, C_QA, first=j)
                load_x(j + 1)
            load_group(w_in_p, PG, N_QK, C_QA, first=LEAD)
            load_group(w_in_p, PG, N_QK + PG, C_QA + GROUP)
            for u in range(2):
                load_group(w_in_p, PG, N_QK + 16 + u * PG, C_QA + WIDTH + u * GROUP)
            with sp.Fori(0, 2) as b:
                for u in range(2):
                    load_group(w_in_p, PG, N_QK + 32 + b * 16 + u * PG, C_QB + b * WIDTH + u * GROUP)
            with sp.Fori(0, 2) as a:
                for u in range(2):
                    load_group(w_in_p, PG, N_V + a * 16 + u * PG, C_VA + a * (C_VB - C_VA) + u * GROUP)
            with sp.Fori(0, 8) as g:
                load_group(w_in_p, PG, N_GATE + g * PG, C_GATE + g * GROUP)
            with sp.Fori(0, 4) as c:
                load_group(w_b_p, PB, N_BRANCH + c * 8, c * GROUP)
                load_group(w_a_p, PB, N_BRANCH + c * 8 + PB, c * GROUP)
            with sp.Fori(0, 4) as c:
                load_group(w_out_p, PG, N_OUT + c * PG, c * GROUP)
            with sp.Fori(0, PAIRS_UP) as i:
                load_group(w_up_p, PG, N_UP + i * 16, i * GROUP)
                load_group(w_up_p, PG, N_UP + i * 16 + PG, D_FF + i * GROUP)
            with sp.Fori(0, 2) as i:
                for u in range(2):
                    load_group(w_down_p, PF, N_DOWN + i * 2 * PF + u * PF, i * 2 * GROUP + u * GROUP,
                               slot0=u * PF % RING)
            for n, (t, q) in enumerate(BLOCKS_VECTOR):
                sp.wait_ge(out_ready, n + 1)
                sp.dma_start(out[0, t * P:(t + 1) * P, q * 512:(q + 1) * 512],
                             res[:, t, q * 512:(q + 1) * 512]).then_inc(out_stored, 16)
            sp.wait_ge(out_stored, 8 * 16)

        @block.gpsimd
        def _(pool):
            pool.memset(ident[:, :], 0.0).then_inc(pool_steps, 1)
            pool.wait_ge(pool_steps, 1)
            pool.affine_select(out=ident[:, :], in_=ident[:, :], compare_op=ALU.not_equal, fill=1.0,
                               base=0, pattern=[[-1, P]], channel_multiplier=1).then_inc(ident_ready, 1)
            pool.memset(ones[:, :], 1.0 / HEAD).then_inc(ones_ready, 1)
            pool.iota(dist[:, :], pattern=[[-1, 384]], base=P, channel_multiplier=1,
                      allow_small_or_imprecise_dtypes=True).then_inc(dist_raw, 1)
            rows = lambda v: v.rearrange("(c p) -> c p", p=P)
            pool.dma_start(par[0:80, 0, :], rows(b_in[0])).then_inc(par_loaded, 16)
            pool.dma_start(par[80:96, 0, :], rows(ln1_g[0])).then_inc(par_loaded, 16)
            pool.dma_start(par[96:112, 0, :], rows(ln1_b[0])).then_inc(par_loaded, 16)
            for k in range(3):
                pool.dma_start(par[0:88, 1 + k, :], rows(conv_w[0, k])).then_inc(par_loaded, 16)
            pool.dma_start(par[0:88, 4, :], rows(conv_b[0])).then_inc(par_loaded, 16)
            for k, v in enumerate((lam_q1, lam_q2, lam_k1, lam_k2)):
                pool.dma_start(lamv[:, k, :], v[0].partition_broadcast(P)).then_inc(lam_loaded, 16)
            pool.dma_start(subg, subln_g[0].rearrange("(p a) -> p a", a=1)).then_inc(lam_loaded, 16)
            for s, c in enumerate((C_VA, C_VB)):
                pool.dma_start(vbias[:, s, :], b_in[0, c:c + WIDTH].partition_broadcast(P)
                               ).then_inc(vbias_loaded, 16)
            pool.wait_ge(xt_ready, KC // 2)
            for b in range(2):
                for h in range(HEADS):
                    src = bass.AP(rpb.tensor,
                                  h * RPB_R * RPB_C + (5 - b) * RPB_C + NA_KC - 1 - (GRID_W - 1),
                                  [[1, GRID_W], [RPB_C, 6], [1, GRID_W]])
                    pool.dma_start(rel[b * 64:(b + 1) * 64, h], src).then_inc(rel_loaded, 16)
            pool.wait_ge(rel_loaded, 16 * 2 * HEADS)
            for b in range(2):
                if b:
                    pool.wait_ge(rel_masked, 1)
                lo = rel[b * 64:(b + 1) * 64, :, :, 0:48].rearrange("p h j c -> p (h j) c")
                pool.affine_select(out=lo, in_=lo, compare_op=ALU.is_ge, fill=MASKED,
                                   base=8 - (GRID_W - 1), pattern=[[0, 6 * HEADS], [1, 48]],
                                   channel_multiplier=1).then_inc(rel_masked, 1)
            for b in range(2):
                pool.wait_ge(rel_masked, 2 + b)
                hi = rel[b * 64:(b + 1) * 64, :, :, 16:64].rearrange("p h j c -> p (h j) c")
                pool.affine_select(out=hi, in_=hi, compare_op=ALU.is_ge, fill=MASKED,
                                   base=GRID_W - 1 + 7 - 16, pattern=[[0, 6 * HEADS], [-1, 48]],
                                   channel_multiplier=-1).then_inc(rel_masked, 1)
            pool.wait_ge(rel_masked, 4)
            pool.wait_ge(banks_free, evacuated(G_V - 1))
            with pool.Fori(0, HEADS) as h:
                pool.wait_ge(scores_ready, START + h * 3)
                for k in range(2):
                    pool.tensor_copy(stA[:, k, :], qkT[:, k, bass.ds(h, 1), :].rearrange("p a s -> p (a s)")
                                     ).then_inc(staged_qk, 1)
                pool.tensor_copy(stQb[:, :], qkT[:, 2, bass.ds(h, 1), :].rearrange("p a s -> p (a s)")
                                 ).then_inc(staged_qk, 1)
                pool.wait_ge(banks_free, evacuated(G_GATE - 1))
                pool.wait_ge(pv_done, START + h * 2)
                for k in range(2):
                    pool.tensor_copy(stV[:, k], vN[:, :, k, bass.ds(h * HEAD, HEAD)]
                                     ).then_inc(staged_v, 1)
            pool.wait_ge(staged_v, 2 * HEADS)
            pool.wait_ge(staged_qk, 3 * HEADS)
            pool.dma_start(res[:, :, :], x[0].rearrange("(t p) d -> p t d", p=P)).then_inc(res_loaded, 16)
            pool.wait_ge(oa_lo, START + HEADS)
            pool.dma_start(ln1_nat[:, 0, :], ln1_g[0].partition_broadcast(P)).then_inc(ln1_loaded, 16)
            pool.dma_start(ln1_nat[:, 1, :], ln1_b[0].partition_broadcast(P)).then_inc(ln1_loaded, 16)
            pool.wait_ge(ln_steps, 8)
            for q in range(2, 4):
                part = res[:, 1, q * 512:(q + 1) * 512]
                pool.tensor_scalar(part, part, rstd[:, 1:2], shift[:, 1:2], ALU.mult, ALU.add
                                   ).then_inc(xn1_rest_ready, 1)
            pool.wait_ge(ln1_loaded, 32)
            pool.wait_ge(x1t_turned, KC // 2)
            for t in range(TT):
                pool.tensor_tensor(res[:, t, :], res[:, t, :], ln1_nat[:, 0, :], ALU.mult
                                   ).then_inc(x1_nat, 1)
            for t in range(TT):
                pool.wait_ge(x1_nat, t + 1)
                pool.tensor_tensor(res[:, t, :], res[:, t, :], ln1_nat[:, 1, :], ALU.add
                                   ).then_inc(x1_nat, 1)
            pool.wait_ge(used, RING + N_DOWN)
            pool.dma_start(ln2_nat[:, 0, :], ln2_g[0].partition_broadcast(P)).then_inc(ln2_loaded, 16)
            pool.dma_start(ln2_nat[:, 1, :], ln2_b[0].partition_broadcast(P)).then_inc(ln2_loaded, 16)
            pool.wait_ge(ln2_loaded, 32)
            for n, (t, q) in enumerate(BLOCKS_SHARED):
                cols = slice(q * 512, (q + 1) * 512)
                pool.wait_ge(shared_normed, n + 1)
                pool.tensor_tensor(res[:, t, cols], res[:, t, cols], ln2_nat[:, 0, cols], ALU.mult
                                   ).then_inc(shared_steps, 1)
                pool.wait_ge(shared_steps, 2 * n + 1)
                pool.tensor_tensor(res[:, t, cols], res[:, t, cols], ln2_nat[:, 1, cols], ALU.add
                                   ).then_inc(shared_steps, 1)

        @block.tensor
        def _(pe):
            def three(acc, w, a, first, last):
                pe.matmul(acc, w[0], a[0], start=first, stop=False, skip_group_check=True)
                pe.matmul(acc, w[0], a[1], start=False, stop=False, skip_group_check=True)
                return pe.matmul(acc, w[1], a[0], start=False, stop=last, skip_group_check=True)

            def piece_feature_major(n, slot, j, count, bank, act_hi, act_lo):
                pe.wait_ge(residual, n + RING + 1)
                for a in range(PIECE_K):
                    k = j * PIECE_K + a
                    for s in range(SUB):
                        mm = three(ps[:, bank + s // 2, (s % 2) * SEQ:(s % 2 + 1) * SEQ],
                                   (w_hi[:, slot, a, s * P:(s + 1) * P], w_lo[:, slot, a, s * P:(s + 1) * P]),
                                   (act_hi[:, k, :], act_lo[:, k, :]),
                                   k == 0 and s % 2 == 0, k == count * PIECE_K - 1)
                mm.then_inc(used, 1)

            def piece_token_major(n, slot, j, count, bank, act_hi, act_lo):
                pe.wait_ge(residual, n + RING + 1)
                for t in range(TT):
                    for a in range(PIECE_K):
                        k = j * PIECE_K + a
                        acc = ps[:, bank + t, :]
                        hi, lo = act_hi[:, k, t * P:(t + 1) * P], act_lo[:, k, t * P:(t + 1) * P]
                        pe.matmul(acc, hi, w_hi[:, slot, a, :], start=(k == 0), stop=False)
                        pe.matmul(acc, hi, w_lo[:, slot, a, :], start=False, stop=False)
                        mm = pe.matmul(acc, lo, w_hi[:, slot, a, :], start=False,
                                       stop=(k == count * PIECE_K - 1))
                    if t == 0 and j == count - 1:
                        mm.then_inc(tile0_sums, 1)
                mm.then_inc(used, 1)

            def group(piece, n0, count, bank, act_hi, act_lo, slot0=0, between=None):
                for j in range(count):
                    if between:
                        between(j)
                    piece(n0 + j, (slot0 + j) % RING, j, count, bank, act_hi, act_lo)

            pe.sem_inc(used, RING)
            for s in (scores_ready, pv_done):
                pe.sem_inc(s, START)
            def turn_x(b):
                if b % 2 == 0:
                    pe.wait_ge(x_loaded[b // 2], 16)
                for a in range(2):
                    for t in range(TT):
                        k = 2 * b + a
                        mm = pe.transpose(ps[:, b, a * SEQ + t * P:a * SEQ + (t + 1) * P],
                                          x_in[:, t, k * P:(k + 1) * P], ident[:, :])
                mm.then_inc(xt_ready, 1)

            def turn_parameters():
                pe.wait_ge(par_loaded, 16 * 7)
                for c, (r, col) in enumerate(((112, 0), (88, T_CW), (88, T_CW + 88), (88, T_CW + 176),
                                              (88, T_CB))):
                    mm = pe.transpose(ps[:, 3, col:col + r], par[0:r, c, :], ident[0:r, 0:r])
                mm.then_inc(par_turned, 1)

            def first_steps(j):
                if 1 <= j and j + LEAD < KC // 2:
                    turn_x(j + LEAD)
                pe.wait_ge(xt_lo, max(2, j + 1))
                if j == 6:
                    turn_parameters()

            pe.wait_ge(ident_ready, 1)
            for b in range(LEAD + 1):
                turn_x(b)
            group(piece_feature_major, N_QK, PG, 0, xT_hi, xT_lo, between=first_steps)
            pe.wait_ge(table_ready, 1)
            group(piece_feature_major, N_QK + PG, PG, 2, xT_hi, xT_lo)
            with pe.Fori(0, 3) as i:
                for u in range(2):
                    pe.wait_ge(banks_free, G_QK + i * 2 + 2 + u + 1)
                    group(piece_feature_major, N_QK + i * 16 + (2 + u) * PG, PG, 2 * u, xT_hi, xT_lo)
            with pe.Fori(0, 2) as i:
                for u in range(2):
                    pe.wait_ge(banks_free, G_V + i * 2 + u + 1)
                    group(piece_token_major, N_V + i * 16 + u * PG, PG, 2 * u, xT_hi, xT_lo)

            def scores(h):
                pe.wait_ge(staged_qk, h * 3 + 3)
                pe.wait_ge(ob_lo, START + h)
                for t in range(TT):
                    for m in range(2):
                        mm = pe.matmul(ps[:, 4 + m, t * SEQ:(t + 1) * SEQ],
                                       stA[m * 64:(m + 1) * 64, 0, t * P:(t + 1) * P],
                                       stA[m * 64:(m + 1) * 64, 1, :], start=True, stop=True)
                        if t == TT - 1:
                            mm.then_inc(scores_ready, 1)
                for t in range(TT):
                    mm = pe.matmul(ps[:, 6, t * SEQ:(t + 1) * SEQ], stQb[:, t * P:(t + 1) * P],
                                   qkT[:, 3, bass.ds(h, 1), :].rearrange("p a s -> p (a s)"),
                                   start=True, stop=True)
                mm.then_inc(scores_ready, 1)

            def turn_probs(h):
                pe.wait_ge(normed_a, h + 1)
                for c in range(TT):
                    for t in range(TT):
                        mm = pe.transpose(ps[:, 7, c * SEQ + t * P:c * SEQ + (t + 1) * P],
                                          sA[:, 0, t, c * P:(c + 1) * P], ident[:, :])
                mm.then_inc(turned, 1)
                pe.wait_ge(normed_b, h + 1)
                for c in range(TT):
                    for t in range(TT):
                        mm = pe.transpose(ps[:, 6, c * SEQ + t * P:c * SEQ + (t + 1) * P],
                                          sB[:, t, c * P:(c + 1) * P], ident[:, :])
                mm.then_inc(turned, 1)

            def values(h):
                pe.wait_ge(staged_v, h * 2 + 2)
                for k, (probs, ready) in enumerate(((aT, aT_ready), (pT, pT_ready))):
                    pe.wait_ge(ready, h + 1)
                    for c in range(TT):
                        mm = pe.matmul(ps[:, 4 + 2 * k, 0:SEQ], stV[:, k, c, :], probs[:, c, :],
                                       start=(c == 0), stop=(c == TT - 1))
                    mm.then_inc(pv_done, 1)

            def mean_squares(h):
                pe.wait_ge(squared, h + 1)
                pe.matmul(ps[:, 7, 0:SEQ], ones[:, :], oa_sq, start=True, stop=True).then_inc(ms_ready, 1)

            pe.wait_ge(ones_ready, 1)
            with pe.Fori(0, 4) as i:
                for u in range(2):
                    h = i * 2 + u
                    steps = {0: scores, 4: turn_probs, 6: values, 7: mean_squares}
                    pe.wait_ge(banks_free, G_GATE + i * 2 + u + 1)
                    group(piece_feature_major, N_GATE + i * 16 + u * PG, PG, 2 * u, xT_hi, xT_lo,
                          between=lambda j: steps[j](h) if j in steps else None)

            pe.wait_ge(banks_free, evacuated(G_END - 2))
            pe.wait_ge(ob_lo, START + HEADS)
            with pe.Fori(0, 4) as c:
                pe.wait_ge(b_gated, START + c * 2)
                group(piece_feature_major, N_BRANCH + c * 8, PB, 0, obT_hi, obT_lo)
                pe.wait_ge(banks_free, evacuated(G_END - 1))
                pe.wait_ge(oa_lo, START + HEADS)
                pe.wait_ge(a_gated, START + c * 2)
                group(piece_feature_major, N_BRANCH + c * 8 + PB, PB, 2, oaT_hi, oaT_lo)
            pe.wait_ge(b_gated, START + 8)
            with pe.Fori(0, 2) as i:
                for u in range(2):
                    pe.wait_ge(res_steps, START + i * (2 + 2 * u))
                    group(piece_token_major, N_OUT + i * 16 + u * PG, PG, 2 * u, yT_hi, yT_lo,
                          between=lambda j: pe.wait_ge(y_lo, START + (8 if u else j + 1)))

            def turn_x1(b):
                if b % 2 == 0:
                    q = b // 2
                    pe.wait_ge(xn0_ready, q + 1)
                    pe.wait_ge(xn1_ready if q < 2 else xn1_rest_ready, q % 2 + 1)
                for a in range(2):
                    for t in range(TT):
                        k = 2 * b + a
                        mm = pe.transpose(ps[:, b, a * SEQ + t * P:a * SEQ + (t + 1) * P],
                                          res[:, t, k * P:(k + 1) * P], ident[:, :])
                mm.then_inc(x1t_turned, 1)

            def x1_steps(j):
                if 1 <= j and j + LEAD + 2 < KC // 2:
                    turn_x1(j + LEAD + 2)
                pe.wait_ge(x1_lo, max(2, j + 1))

            for b in range(LEAD + 3):
                turn_x1(b)
            def up(i, u, between=None):
                pe.wait_ge((g_conv, v_conv)[u], START + i * 2 * SUB)
                group(piece_feature_major, N_UP + i * 16 + u * PG, PG, 2 * u, x1T_hi, x1T_lo,
                      between=between)

            up(0, 0, between=x1_steps)
            with pe.Fori(0, PAIRS_UP - 1) as i:
                up(i, 1)
                up(i + 1, 0)
            up(PAIRS_UP - 1, 1)
            with pe.Fori(0, 2) as i:
                for u in range(2):
                    pe.wait_ge((g_conv, v_conv)[u], START + PAIRS_UP * 2 * SUB)
                    pe.wait_ge(res_steps, START + i * (10 + 2 * u))
                    group(piece_token_major, N_DOWN + i * 2 * PF + u * PF, PF, 2 * u, hT_hi, hT_lo,
                          slot0=u * PF % RING,
                          between=lambda j: pe.wait_ge(h_lo, START + 2 * j + 2))

        @block.scalar
        def _(act):
            def round_piece(c, off4=0):
                slot = c % RING
                act.wait_ge(raw_loaded[slot], off4 * 16 + 16 * (c // RING + 1))
                act.wait_ge(used, off4 * RING + c + 1)
                act.activation(w_hi[:, slot], raw[:, slot], ACT.Copy).then_inc(rounded, 1)

            def rounds(c, count, off4=0, between=None):
                for j in range(count):
                    round_piece(c + j + LEAD, off4)
                    if between:
                        between(j)

            act.sem_inc(banks_free, 2)
            act.wait_ge(dist_raw, 1)
            act.activation(dist[:, :], dist[:, :], ACT.Abs).then_inc(dist_ready, 1)
            def high_x(b):
                act.wait_ge(xt_ready, b + 1)
                act.activation(xT_hi[:, 2 * b:2 * b + 2, :], ps[:, b, :].rearrange("p (a s) -> p a s", a=2),
                               ACT.Copy).then_inc(xt_hi, 1)

            def first_steps(j):
                if j + LEAD + 1 < KC // 2:
                    high_x(j + LEAD + 1)
                if j == 5:
                    act.wait_ge(lam_steps, 2)
                    act.activation(lam_exp, lam_dot, ACT.Exp).then_inc(lam_exped, 1)
                if j == 6:
                    act.wait_ge(par_turned, 1)
                    act.activation(table[:, :], ps[:, 3, 0:T_ALL], ACT.Copy).then_inc(table_ready, 1)
                    act.wait_ge(table_ready, 1)

            high_x(0)
            for c in range(LEAD):
                high_x(c + 1)
                round_piece(c)

            def reverse_rows(tokens):
                return tokens.rearrange("p (r c) -> p r c", c=GRID_W)[:, :, ::-1]

            def evacuate_columns(n_end, off4, bank, dst, dst0, col0, reverse=False):
                act.wait_ge(used, off4 * RING + RING + n_end)
                for s in range(SUB):
                    into = dst[:, bass.ds(dst0 + s, 1), :].rearrange("p a s -> p (a s)")
                    sums_s = ps[:, bank + s // 2, (s % 2) * SEQ:(s % 2 + 1) * SEQ]
                    if reverse:
                        into = into.rearrange("p (r c) -> p r c", c=GRID_W)
                        sums_s = reverse_rows(sums_s)
                    ev = act.activation(into, sums_s, ACT.Identity, bias=table[:, bass.ds(col0 + s, 1)])
                ev.then_inc(banks_free, 1)

            qk_chunks = qkT[:, :, :, :].rearrange("p k h s -> p (k h) s")

            def q_or_k(kind, off4, col, between=None, reverse=False):
                for u in range(2):
                    rounds(N_QK + u * PG, PG, off4, between=None if u else between)
                    evacuate_columns(N_QK + (u + 1) * PG, off4, 2 * u, qk_chunks,
                                     kind * HEADS + u * SUB, T_BIN + col + u * SUB, reverse)

            q_or_k(0, 0, C_QA // P, between=first_steps)
            q_or_k(1, 4, (C_QA + WIDTH) // P)
            q_or_k(2, 8, C_QB // P, reverse=True)
            q_or_k(3, 12, (C_QB + WIDTH) // P)
            with act.Fori(0, 4) as i:
                rounds(N_V, PG, i * 2)

            def exponentials(h):
                act.wait_ge(maxed, h * 3 + 3)
                for m in range(2):
                    for t in range(TT):
                        k = m * TT + t
                        act.activation(sA[:, m, t, :], sA[:, m, t, :], ACT.Exp, scale=DIFF_SCALE,
                                       bias=neg_maxs[:, k:k + 1], accum_out=sums[:, k:k + 1]
                                       ).then_inc(exped, 1)
                for t in range(TT):
                    act.activation(sB[:, t, :], sB[:, t, :], ACT.Exp, bias=neg_max[:, 4 + t:5 + t],
                                   accum_out=sums[:, 4 + t:5 + t]).then_inc(exped, 1)

            def copy_pT(h):
                act.wait_ge(turned, h * 2 + 2)
                act.activation(pT[:, :, :].rearrange("p k (r c) -> p (k r) c", c=GRID_W),
                               reverse_rows(ps[:, 6, :]), ACT.Copy).then_inc(pT_ready, 1)

            def read_values(h):
                act.wait_ge(oa_copied, h + 1)
                act.activation(oa_sq, oa, ACT.Square).then_inc(squared, 1)
                act.wait_ge(pv_done, START + h * 2 + 2)
                act.activation(obT_hi[:, bass.ds(h, 1), :].rearrange("p a s -> p (a s)"),
                               ps[:, 6, 0:SEQ], ACT.Copy).then_inc(ob_hi, 1)

            def finish_a(h):
                act.wait_ge(ms_ready, h + 1)
                act.activation(oa_rms, ps[:, 7, 0:SEQ], ACT.Sqrt, bias=eps_c).then_inc(oa_sqrt, 1)
                act.wait_ge(oa_steps, h * 2 + 2)
                act.activation(oaT_hi[:, bass.ds(h, 1), :].rearrange("p a s -> p (a s)"), oa, ACT.Copy
                               ).then_inc(oa_hi, 1)

            act.wait_ge(banks_free, evacuated(G_GATE - 1))
            with act.Fori(0, 4) as i:
                for u in range(2):
                    h = i * 2 + u
                    steps = {1: exponentials, 4: copy_pT, 6: read_values, 7: finish_a}
                    rounds(N_GATE + u * PG, PG, i * 4,
                           between=lambda j: steps[j](h) if j in steps else None)
                    evacuate_columns(N_GATE + (u + 1) * PG, i * 4, 2 * u, gate,
                                     i * 8 + u * SUB, T_BIN + C_GATE // P + i * 8 + u * SUB)
            def gates_of(c):
                act.wait_ge(banks_free, evacuated(G_END - 1))
                for k in range(2):
                    part = gate[:, bass.ds(k * KC + c * SUB, SUB), :]
                    act.activation(part, part, ACT.Sigmoid).then_inc(gates_on, 1)

            def high_y(c, j):
                if j == 1:
                    for pair in range(2):
                        act.wait_ge(y_summed, c * 2 + 1 + pair)
                        chunk = c * SUB + 2 * pair
                        act.activation(yT_hi[:, bass.ds(chunk, 2), :], gate[:, bass.ds(chunk, 2), :],
                                       ACT.Copy).then_inc(y_hi, 1)

            rounds(N_BRANCH, PB, between=lambda j: gates_of(0) if j == 2 else None)
            with act.Fori(0, 3) as c:
                rounds(N_BRANCH + PB, PB, c * 2)
                rounds(N_BRANCH + 2 * PB, PB, c * 2,
                       between=lambda j: gates_of(c + 1) if j == 2 else high_y(c, j))
            rounds(N_OUT - PB, PB)
            rounds(N_OUT, PG, between=lambda j: high_y(3, j))
            with act.Fori(0, 3) as i:
                rounds(N_OUT + PG, PG, i * 2)
            def norm_tile0(k, blocks, done):
                def root(t):
                    act.wait_ge(ln_steps, 8 * k + 4 * t + 2)
                    act.activation(std[:, t:t + 1], vpe[:, t:t + 1], ACT.Sqrt).then_inc(ln_sqrt, 1)

                root(0)
                act.wait_ge(ln_steps, 8 * k + 4)
                for q in range(blocks):
                    part = res[:, 0, q * 512:(q + 1) * 512]
                    act.activation(part, part, ACT.Identity, scale=rstd[:, 0:1], bias=shift[:, 0:1]
                                   ).then_inc(done, 1)
                    if q == 0:
                        root(1)

            norm_tile0(0, 4, xn0_ready)

            def high_x1(b):
                act.wait_ge(x1_aff, b + 1)
                k = 2 * b + 1
                act.activation(x1f[:, b % 4, SEQ:2 * SEQ], ps[:, b, SEQ:2 * SEQ], ACT.Identity,
                               scale=table[:, T_LNG + k:T_LNG + k + 1],
                               bias=table[:, T_LNB + k:T_LNB + k + 1]).then_inc(x1_aff2, 1)
                act.wait_ge(x1_aff2, b + 1)
                act.activation(x1T_hi[:, 2 * b:2 * b + 2, :],
                               x1f[:, b % 4, :].rearrange("p (a s) -> p a s", a=2), ACT.Copy
                               ).then_inc(x1_hi, 1)

            for b in range(LEAD + 1):
                high_x1(b)

            def mid(i, s, dst, bank, first, done):
                act.activation(dst[:, s, :], ps[:, bank + s // 2, (s % 2) * SEQ:(s % 2 + 1) * SEQ],
                               ACT.Identity, bias=table[:, bass.ds(T_CB + first + i * SUB + s, 1)],
                               scale=table[:, bass.ds(T_CW + 88 + first + i * SUB + s, 1)]
                               ).then_inc(done, 1)

            def gate_steps(i, j):
                if j == 0:
                    act.wait_ge(used, i * 16 + RING + N_UP + PG)
                    act.wait_ge(h_lo, START + i * SUB)
                if j in (0, 1):
                    for s in (2 * j, 2 * j + 1):
                        mid(i, s, cg, 0, 0, g_mid)
                if j in (3, 4):
                    for s in (2 * j - 6, 2 * j - 5):
                        act.wait_ge(g_conv, START + i * 2 * SUB + 4 * (j - 2))
                        act.activation(cg[:, s, :], cg[:, s, :], ACT.Gelu).then_inc(g_act, 1)

            def value_steps(i, j):
                if j == 0:
                    act.wait_ge(used, i * 16 + RING + N_UP + 2 * PG)
                    act.wait_ge(h_ready, START + i * SUB)
                if j in (0, 1):
                    for s in (2 * j, 2 * j + 1):
                        mid(i, s, cv, 2, FC, v_mid)
                if j in (4, 5):
                    for s in (2 * j - 8, 2 * j - 7):
                        act.wait_ge(h_ready, START + i * SUB + s + 1)
                        act.activation(hT_hi[:, bass.ds(i * SUB + s, 1), :].rearrange("p a s -> p (a s)"),
                                       cg[:, s, :], ACT.Copy).then_inc(h_hi, 1)

            rounds(N_UP, PG, between=lambda j: high_x1(j + LEAD + 1) if j + LEAD + 1 < KC // 2 else None)
            last = PAIRS_UP - 1
            with act.Fori(0, last) as i:
                rounds(N_UP + PG, PG, i * 4, between=lambda j: gate_steps(i, j))
                rounds(N_UP + 2 * PG, PG, i * 4, between=lambda j: value_steps(i, j))
            rounds(N_UP + PG, PG, last * 4, between=lambda j: gate_steps(last, j))
            rounds(N_DOWN, PG, 0, between=lambda j: value_steps(last, j))
            with act.Fori(0, 9) as i:
                rounds(N_DOWN + PG, 8, i * 2)
            rounds(N_DOWN + PG + 72, 88 - PG - 72 - LEAD)
            norm_tile0(1, len(BLOCKS_SHARED), shared_normed)
            for n, (t, q) in enumerate(BLOCKS_SHARED):
                act.wait_ge(shared_steps, 2 * n + 2)
                act.dma_start(out[0, t * P:(t + 1) * P, q * 512:(q + 1) * 512],
                              res[:, t, q * 512:(q + 1) * 512]).then_inc(out_stored, 16)

        @block.vector
        def _(dve):
            def split_piece(c, off4=0):
                slot = c % RING
                dve.wait_ge(rounded, off4 * RING + c + 1)
                dve.tensor_tensor(w_lo[:, slot], raw[:, slot], w_hi[:, slot].bitcast(F32), ALU.subtract
                                  ).then_inc(residual, 1)

            def splits(c, count, off4=0, between=None, before=None):
                for j in range(count):
                    if before:
                        before(j)
                    split_piece(c + j + LEAD, off4)
                    if between:
                        between(j)

            dve.sem_inc(residual, RING)
            for s in (ob_lo, oa_lo, b_gated, a_gated, y_lo, res_steps, g_conv, v_conv, h_ready, h_lo):
                dve.sem_inc(s, START)
            for h in range(HEADS):
                dve.memset(slope8[:, h:h + 1], -(2.0 ** -(h + 1)) / DIFF_SCALE).then_inc(consts_set, 1)
            dve.memset(eps_c, RMS_EPS).then_inc(consts_set, 1)
            def low_x(b):
                dve.wait_ge(xt_hi, b + 1)
                dve.tensor_tensor(xT_lo[:, 2 * b:2 * b + 2, :],
                                  ps[:, b, :].rearrange("p (a s) -> p a s", a=2),
                                  xT_hi[:, 2 * b:2 * b + 2, :].bitcast(F32), ALU.subtract
                                  ).then_inc(xt_lo, 1)

            def first_steps(j):
                if j + LEAD + 1 < KC // 2:
                    low_x(j + LEAD + 1)
                if j == 4:
                    dve.wait_ge(lam_loaded, 16 * 5)
                    dve.tensor_tensor(lamv[:, 0:2, :], lamv[:, 0:2, :], lamv[:, 2:4, :], ALU.mult
                                      ).then_inc(lam_steps, 1)
                    dve.wait_ge(lam_steps, 1)
                    dve.tensor_reduce(lam_dot, lamv[:, 0:2, :], AX.X, ALU.add).then_inc(lam_steps, 1)
                    dve.tensor_scalar(subg8, subg, 1.0 - LAMBDA_INIT, None, ALU.mult).then_inc(lam_steps, 1)
                if j == 7:
                    dve.wait_ge(lam_exped, 1)
                    dve.tensor_tensor(lam_dif, lam_exp[:, 1:2], lam_exp[:, 0:1], ALU.subtract
                                      ).then_inc(lam_steps, 1)
                    dve.wait_ge(lam_steps, 4)
                    dve.tensor_scalar(neg_lam, lam_dif, -LAMBDA_INIT, None, ALU.add).then_inc(lam_steps, 1)

            low_x(0)
            for c in range(LEAD):
                low_x(c + 1)
                split_piece(c)
            splits(N_QK, PG, between=first_steps)
            with dve.Fori(0, 7) as i:
                splits(N_QK + PG, PG, i * 2)

            dve.wait_ge(vbias_loaded, 32)
            dve.wait_ge(banks_free, evacuated(G_V - 1))
            with dve.Fori(0, 2) as i:
                for u in range(2):
                    splits(N_V + u * PG, PG, i * 4)
                    dve.wait_ge(used, i * 16 + RING + N_V + (u + 1) * PG)
                    for t in range(TT):
                        ev = dve.tensor_tensor(
                            vN[:, t, bass.ds(i, 1), u * GROUP:(u + 1) * GROUP].rearrange("p a n -> p (a n)"),
                            ps[:, 2 * u + t, :],
                            vbias[:, bass.ds(i, 1), u * GROUP:(u + 1) * GROUP].rearrange("p a n -> p (a n)"),
                            ALU.add)
                    ev.then_inc(banks_free, 1)

            def bias_and_max(h):
                dve.wait_ge(oa_lo, START + h)
                for m in range(2):
                    dve.wait_ge(scores_ready, START + h * 3 + m + 1)
                    for t in range(TT):
                        dve.scalar_tensor_tensor(
                            sA[:, m, t, :], dist[:, P - t * P:P - t * P + SEQ], slope8[:, bass.ds(h, 1)],
                            ps[:, 4 + m, t * SEQ:(t + 1) * SEQ], ALU.mult, ALU.add).then_inc(biased, 1)
                dve.wait_ge(scores_ready, START + h * 3 + 3)
                for t in range(TT):
                    dve.scalar_tensor_tensor(
                        sB[:, t, :], ps[:, 6, t * SEQ:(t + 1) * SEQ], NA_SCALE,
                        rel[:, bass.ds(h, 1), 2 - 2 * t:6 - 2 * t, :].rearrange("p a j c -> p (a j c)"),
                        ALU.mult, ALU.add).then_inc(biased, 1)
                dve.wait_ge(biased, h * 6 + 4)
                dve.tensor_reduce(neg_max[:, 0:4], sA[:, :, :, :].rearrange("p m t s -> p (m t) s"), AX.X,
                                  ALU.max, negate=True).then_inc(maxed, 1)
                dve.wait_ge(biased, h * 6 + 6)
                dve.tensor_reduce(neg_max[:, 4:6], sB[:, :, :], AX.X, ALU.max, negate=True
                                  ).then_inc(maxed, 1)
                dve.wait_ge(maxed, h * 3 + 1)
                dve.tensor_scalar(neg_maxs, neg_max[:, 0:4], DIFF_SCALE, None, ALU.mult
                                  ).then_inc(maxed, 1)

            def normalise(h):
                dve.wait_ge(exped, h * 6 + 6)
                dve.reciprocal(rsum, sums).then_inc(soft, 1)
                dve.wait_ge(soft, h * 4 + 1)
                dve.tensor_scalar(coef, rsum[:, 2:4], neg_lam, None, ALU.mult).then_inc(soft, 1)
                for t in range(TT):
                    dve.tensor_scalar(sA[:, 0, t, :], sA[:, 0, t, :], rsum[:, t:t + 1], None, ALU.mult
                                      ).then_inc(soft, 1)
                for t in range(TT):
                    op = dve.tensor_scalar(sB[:, t, :], sB[:, t, :], rsum[:, 4 + t:5 + t], None, ALU.mult)
                op.then_inc(normed_b, 1)
                dve.wait_ge(soft, h * 4 + 4)
                for t in range(TT):
                    op = dve.scalar_tensor_tensor(sA[:, 0, t, :], sA[:, 1, t, :], coef[:, t:t + 1],
                                                  sA[:, 0, t, :], ALU.mult, ALU.add)
                op.then_inc(normed_a, 1)

            def copy_aT(h):
                dve.wait_ge(turned, h * 2 + 1)
                dve.tensor_copy(aT[:, :, :], ps[:, 7, :].rearrange("p (c s) -> p c s", c=TT)
                                ).then_inc(aT_ready, 1)

            def read_values(h):
                dve.wait_ge(pv_done, START + h * 2 + 1)
                dve.tensor_copy(oa, ps[:, 4, 0:SEQ]).then_inc(oa_copied, 1)
                dve.wait_ge(ob_hi, h + 1)
                dve.tensor_tensor(obT_lo[:, bass.ds(h, 1), :].rearrange("p a s -> p (a s)"),
                                  ps[:, 6, 0:SEQ],
                                  obT_hi[:, bass.ds(h, 1), :].bitcast(F32).rearrange("p a s -> p (a s)"),
                                  ALU.subtract).then_inc(ob_lo, 1)

            def finish_a(h):
                dve.wait_ge(oa_sqrt, h + 1)
                dve.reciprocal(oa_rms, oa_rms).then_inc(oa_steps, 1)
                dve.wait_ge(oa_steps, h * 2 + 1)
                dve.scalar_tensor_tensor(oa, oa, subg8, oa_rms, ALU.mult, ALU.mult).then_inc(oa_steps, 1)
                dve.wait_ge(oa_hi, h + 1)
                dve.tensor_tensor(oaT_lo[:, bass.ds(h, 1), :].rearrange("p a s -> p (a s)"), oa,
                                  oaT_hi[:, bass.ds(h, 1), :].bitcast(F32).rearrange("p a s -> p (a s)"),
                                  ALU.subtract).then_inc(oa_lo, 1)

            dve.wait_ge(dist_ready, 1)
            dve.wait_ge(rel_masked, 4)
            dve.wait_ge(consts_set, HEADS + 1)
            dve.wait_ge(lam_steps, 5)
            with dve.Fori(0, 4) as i:
                for u in range(2):
                    h = i * 2 + u
                    steps = {1: normalise, 4: copy_aT, 6: read_values, 7: finish_a}
                    splits(N_GATE + u * PG, PG, i * 4,
                           before=lambda j: bias_and_max(h) if j == 0 else None,
                           between=lambda j: steps[j](h) if j in steps else None)
            def gated(c, k, pair):
                chunk = k * KC + c * SUB + 2 * pair
                dve.tensor_tensor(gate[:, bass.ds(chunk, 2), :],
                                  ps[:, 2 - 2 * k + pair, :].rearrange("p (a s) -> p a s", a=2),
                                  gate[:, bass.ds(chunk, 2), :], ALU.mult
                                  ).then_inc(b_gated if k else a_gated, 1)

            def gate_b(c, j):
                if j == 0:
                    dve.wait_ge(gates_on, c * 2 + 2)
                    dve.wait_ge(used, c * 8 + RING + N_BRANCH + PB)
                    for pair in range(2):
                        gated(c, 1, pair)

            def sum_branches(c, j):
                if j == 0:
                    dve.wait_ge(used, c * 8 + RING + N_BRANCH + 2 * PB)
                    for pair in range(2):
                        gated(c, 0, pair)
                    for pair in range(2):
                        dve.wait_ge(b_gated, START + c * 2 + pair + 1)
                        dve.wait_ge(a_gated, START + c * 2 + pair + 1)
                        chunk = c * SUB + 2 * pair
                        dve.tensor_tensor(gate[:, bass.ds(chunk, 2), :], gate[:, bass.ds(chunk, 2), :],
                                          gate[:, bass.ds(chunk + KC, 2), :], ALU.add
                                          ).then_inc(y_summed, 1)
                if j == 1:
                    for pair in range(2):
                        chunk = c * SUB + 2 * pair
                        dve.wait_ge(y_hi, c * 2 + pair + 1)
                        dve.tensor_tensor(yT_lo[:, bass.ds(chunk, 2), :], gate[:, bass.ds(chunk, 2), :],
                                          yT_hi[:, bass.ds(chunk, 2), :].bitcast(F32), ALU.subtract
                                          ).then_inc(y_lo, 1)

            splits(N_BRANCH, PB)
            with dve.Fori(0, 3) as c:
                splits(N_BRANCH + PB, PB, c * 2, between=lambda j: gate_b(c, j))
                splits(N_BRANCH + 2 * PB, PB, c * 2, between=lambda j: sum_branches(c, j))
            splits(N_OUT - PB, PB, between=lambda j: gate_b(3, j))

            def read_out(q, bank, n_end, steps0):
                dve.wait_ge(used, RING + n_end)
                for t in range(TT):
                    part = res[:, t, bass.ds(q * GROUP, GROUP)]
                    dve.scalar_tensor_tensor(part, part, ALPHA, ps[:, bank + t, :], ALU.mult, ALU.add
                                             ).then_inc(res_steps, 1)
                for t in range(TT):
                    dve.wait_ge(res_steps, START + steps0 + t + 1)
                    dve.bn_stats(stats[:, t, bass.ds(q, 1), :].rearrange("p a s -> p (a s)"),
                                 res[:, t, bass.ds(q * GROUP, GROUP)]).then_inc(stat_steps, 1)

            def read_out_last(k, q, bank, n_end, steps0):
                def summed(t):
                    part = res[:, t, q * GROUP:(q + 1) * GROUP]
                    dve.scalar_tensor_tensor(part, part, ALPHA, ps[:, bank + t, :], ALU.mult, ALU.add
                                             ).then_inc(res_steps, 1)

                def statistics(t):
                    dve.wait_ge(res_steps, START + steps0 + t + 1)
                    dve.bn_stats(stats[:, t, q, :], res[:, t, q * GROUP:(q + 1) * GROUP]
                                 ).then_inc(stat_steps, 1)
                    dve.wait_ge(stat_steps, 8 * k + 7 + t)
                    dve.bn_aggr(mv[:, t, :], stats[:, t, :, :].rearrange("p g s -> p (g s)")
                                ).then_inc(ln_steps, 1)
                    dve.wait_ge(ln_steps, 8 * k + 4 * t + 1)
                    dve.tensor_scalar(vpe[:, t:t + 1], mv[:, t, 1:2], LN_EPS, None, ALU.add
                                      ).then_inc(ln_steps, 1)

                def factors(t):
                    dve.wait_ge(ln_sqrt, 2 * k + t + 1)
                    dve.reciprocal(rstd[:, t:t + 1], std[:, t:t + 1]).then_inc(ln_steps, 1)
                    dve.wait_ge(ln_steps, 8 * k + 4 * t + 3)
                    dve.scalar_tensor_tensor(shift[:, t:t + 1], mv[:, t, 0:1], -1.0, rstd[:, t:t + 1],
                                             ALU.mult, ALU.mult).then_inc(ln_steps, 1)

                dve.wait_ge(tile0_sums, 4 * (k + 2))
                summed(0)
                statistics(0)
                dve.wait_ge(used, RING + n_end)
                summed(1)
                factors(0)
                statistics(1)
                factors(1)

            dve.wait_ge(res_loaded, 16)
            splits(N_OUT, PG, between=lambda j: sum_branches(3, j))
            read_out(0, 0, N_OUT + PG, 0)
            for q in range(1, 3):
                splits(N_OUT + q * PG, PG)
                read_out(q, 2 * (q % 2), N_OUT + (q + 1) * PG, q * 2)
            splits(N_OUT + 3 * PG, PG - 1)
            read_out_last(0, 3, 2, N_UP, 6)
            for q in range(2):
                part = res[:, 1, q * 512:(q + 1) * 512]
                dve.tensor_scalar(part, part, mv[:, 1, 0:1], rstd[:, 1:2], ALU.subtract, ALU.mult
                                  ).then_inc(xn1_ready, 1)

            def affine(b):
                dve.wait_ge(x1t_turned, b + 1)
                if b >= 4:
                    dve.wait_ge(x1_lo, b - 3)
                k = 2 * b
                dve.tensor_scalar(x1f[:, b % 4, 0:SEQ], ps[:, b, 0:SEQ],
                                  table[:, T_LNG + k:T_LNG + k + 1], table[:, T_LNB + k:T_LNB + k + 1],
                                  ALU.mult, ALU.add).then_inc(x1_aff, 1)

            def low_x1(b):
                dve.wait_ge(x1_hi, b + 1)
                dve.tensor_tensor(x1T_lo[:, 2 * b:2 * b + 2, :],
                                  x1f[:, b % 4, :].rearrange("p (a s) -> p a s", a=2),
                                  x1T_hi[:, 2 * b:2 * b + 2, :].bitcast(F32), ALU.subtract
                                  ).then_inc(x1_lo, 1)

            affine(0)
            for b in range(LEAD + 1):
                affine(b + 1)
                low_x1(b)
                if b == 1:
                    split_piece(N_UP - 1 + LEAD)

            def x1_steps(j):
                if j + LEAD + 2 < KC // 2:
                    affine(j + LEAD + 2)
                if j + LEAD + 1 < KC // 2:
                    low_x1(j + LEAD + 1)

            def taps(i, j, dst, bank, first, mids, done):
                s0, count = 2 * (j - 1), i * 2 * SUB + 4 * (j - 1)
                dve.wait_ge(mids, i * SUB + s0 + 2)
                for s in (s0, s0 + 1):
                    dve.scalar_tensor_tensor(
                        dst[:, s, 1:SEQ], ps[:, bank + s // 2, (s % 2) * SEQ:(s % 2 + 1) * SEQ - 1],
                        table[:, bass.ds(T_CW + first + i * SUB + s, 1)], dst[:, s, 1:SEQ],
                        ALU.mult, ALU.add).then_inc(done, 1)
                for s in (s0, s0 + 1):
                    dve.wait_ge(done, START + count + s - s0 + 1)
                    dve.scalar_tensor_tensor(
                        dst[:, s, 0:SEQ - 1], ps[:, bank + s // 2, (s % 2) * SEQ + 1:(s % 2 + 1) * SEQ],
                        table[:, bass.ds(T_CW + 176 + first + i * SUB + s, 1)], dst[:, s, 0:SEQ - 1],
                        ALU.mult, ALU.add).then_inc(done, 1)

            def gate_steps(i, j):
                if j in (1, 2):
                    taps(i, j, cg, 0, 0, g_mid, g_conv)

            def value_steps(i, j):
                if j in (1, 2):
                    taps(i, j, cv, 2, FC, v_mid, v_conv)
                if j == 3:
                    dve.wait_ge(v_conv, START + i * 2 * SUB + 2 * SUB)
                    dve.wait_ge(g_act, i * SUB + SUB)
                    for s in range(SUB):
                        dve.tensor_tensor(cg[:, s, :], cg[:, s, :], cv[:, s, :], ALU.mult
                                          ).then_inc(h_ready, 1)
                if j in (5, 6):
                    dve.wait_ge(x1_nat, 2 * TT)
                    for s in (2 * j - 10, 2 * j - 9):
                        chunk = bass.ds(i * SUB + s, 1)
                        dve.wait_ge(h_hi, i * SUB + s + 1)
                        dve.tensor_tensor(hT_lo[:, chunk, :].rearrange("p a s -> p (a s)"), cg[:, s, :],
                                          hT_hi[:, chunk, :].bitcast(F32).rearrange("p a s -> p (a s)"),
                                          ALU.subtract).then_inc(h_lo, 1)

            splits(N_UP, PG, between=x1_steps)
            last = PAIRS_UP - 1
            with dve.Fori(0, last) as i:
                splits(N_UP + PG, PG, i * 4, between=lambda j: gate_steps(i, j))
                splits(N_UP + 2 * PG, PG, i * 4, between=lambda j: value_steps(i, j))
            splits(N_UP + PG, PG, last * 4, between=lambda j: gate_steps(last, j))
            for q in range(4):
                splits(N_DOWN + q * PF, PF if q < 3 else PF - LEAD, 0,
                       between=(lambda j: value_steps(last, j)) if q == 0 else None)
                if q < 3:
                    read_out(q, 2 * (q % 2), N_DOWN + (q + 1) * PF, 8 + q * 2)
            read_out_last(1, 3, 2, N_ALL, 14)
            dve.wait_ge(ln2_loaded, 32)

            def centre(t, q):
                part = res[:, t, q * 512:(q + 1) * 512]
                dve.scalar_tensor_tensor(part, part, mv[:, t, 0:1], ln2_nat[:, 0, q * 512:(q + 1) * 512],
                                         ALU.subtract, ALU.mult).then_inc(out_steps, 1)

            def scale(n, t, q):
                part = res[:, t, q * 512:(q + 1) * 512]
                dve.wait_ge(out_steps, n + 1)
                dve.scalar_tensor_tensor(part, part, rstd[:, t:t + 1], ln2_nat[:, 1, q * 512:(q + 1) * 512],
                                         ALU.mult, ALU.add).then_inc(out_ready, 1)

            centre(*BLOCKS_VECTOR[0])
            for n in range(1, len(BLOCKS_VECTOR)):
                centre(*BLOCKS_VECTOR[n])
                scale(n - 1, *BLOCKS_VECTOR[n - 1])
            scale(len(BLOCKS_VECTOR) - 1, *BLOCKS_VECTOR[-1])


_INS = ["x", "w_in", "b_in", "lam_q1", "lam_k1", "lam_q2", "lam_k2", "subln_g", "rpb", "w_branch_a",
        "w_branch_b", "w_out", "ln1_g", "ln1_b", "w_up", "conv_w", "conv_b", "w_down", "ln2_g", "ln2_b"]


def kernel(**inputs):
    import numpy as _np
    import concourse.bacc as _bacc
    from concourse import mybir as _mybir
    from concourse.bass_utils import run_bass_kernel_spmd as _run

    nc = _bacc.Bacc("TRN2", target_bir_lowering=False, num_devices=1)
    arrays, args = {}, []
    for name in _INS:
        a = _np.ascontiguousarray(inputs[name])
        arrays[f"in_{name}"] = a
        args.append(nc.dram_tensor(f"in_{name}", a.shape, _mybir.dt.from_np(a.dtype), kind="ExternalInput").ap())
    args.append(nc.dram_tensor("out_0", (1, SEQ, D_MODEL), F32, kind="ExternalOutput").ap())
    encoder_block(nc, *args)
    r = _run(nc, [arrays], core_ids=[0])
    return r.results[0]["out_0"]
```
